# Optimizing a Trainium2 kernel written in Bass

```python
import math
import jax, jax.numpy as jnp
from jax import lax
import numpy as np
import jax
import jax.numpy as jnp

D_MODEL = 1024
BATCH = 1
SEQ = 512
DEPTH = 1

HEAD_DIM = 64
FOX_HEADS = 8
NSA_HEADS = 8
NSA_KV_GROUPS = 2
NSA_REP = NSA_HEADS // NSA_KV_GROUPS
CMP_BLOCK = 32
CMP_STRIDE = 16
CMP_HIDDEN = 256
SLC_BLOCK = 64
SLC_TOPK = 16
WINDOW = 512
Q_BLOCK = 128
REL_BUCKETS = 32
REL_MAX_DIST = 128
D_FF = 4 * D_MODEL
RMS_EPS = 1e-6
NEG_INF = -1e30
FORCED_SCORE = 1e4
SCALE = HEAD_DIM ** -0.5

FOX_W = FOX_HEADS * HEAD_DIM
NSA_W = NSA_HEADS * HEAD_DIM
KV_W = NSA_KV_GROUPS * HEAD_DIM
IN_SPLITS = (FOX_W, FOX_W, FOX_W, FOX_HEADS,
             NSA_W, KV_W, KV_W, KV_W, KV_W, KV_W, KV_W, 3 * NSA_HEADS,
             D_MODEL, D_MODEL)
IN_WIDTH = sum(IN_SPLITS)


def rms_norm(x, g):
    xf = x.astype(jnp.float32)
    y = xf * lax.rsqrt(jnp.mean(xf * xf, axis=-1, keepdims=True) + RMS_EPS)
    return (y * g.astype(jnp.float32)).astype(x.dtype)

def masked_softmax(s, mask):
    p = jax.nn.softmax(jnp.where(mask, s, NEG_INF), axis=-1)
    return jnp.where(mask, p, 0.0)

def rel_bucket(dist):
    n = jnp.maximum(dist, 0)
    exact = REL_BUCKETS // 2
    nf = jnp.maximum(n, exact).astype(jnp.float32)
    log_b = exact + (jnp.log(nf / exact) / math.log(REL_MAX_DIST / exact)
                     * (REL_BUCKETS - exact)).astype(jnp.int32)
    return jnp.where(n < exact, n, jnp.minimum(log_b, REL_BUCKETS - 1))

def fox_attention(q, k, v, f_logit, b_f):
    B, T, H, DH = q.shape
    nb = T // Q_BLOCK
    log_f = jax.nn.log_sigmoid(f_logit.astype(jnp.float32) + b_f.astype(jnp.float32))
    c = jnp.cumsum(log_f, axis=1).transpose(0, 2, 1)
    qb = q.reshape(B, nb, Q_BLOCK, H, DH).transpose(1, 0, 3, 2, 4)
    cqb = c.reshape(B, H, nb, Q_BLOCK).transpose(2, 0, 1, 3)
    kpos = jnp.arange(T)

    def block(args):
        i, qi, ci = args
        qpos = i * Q_BLOCK + jnp.arange(Q_BLOCK)
        s = jnp.einsum('bhqd,bkhd->bhqk', qi, k).astype(jnp.float32) * SCALE
        s = s + ci[..., None] - c[:, :, None, :]
        p = masked_softmax(s, kpos[None, :] <= qpos[:, None])
        return jnp.einsum('bhqk,bkhd->bqhd', p.astype(v.dtype), v)

    o = lax.map(block, (jnp.arange(nb), qb, cqb))
    return o.transpose(1, 0, 2, 3, 4).reshape(B, T, H * DH)

def compress_blocks(kv, pe, w1, w2):
    B, T, G, DH = kv.shape
    nc = (T - CMP_BLOCK) // CMP_STRIDE + 1
    idx = np.arange(nc)[:, None] * CMP_STRIDE + np.arange(CMP_BLOCK)[None, :]
    blk = kv[:, idx] + pe[:, None, :]
    blk = blk.transpose(0, 3, 1, 2, 4).reshape(B, G, nc, CMP_BLOCK * DH)
    return jax.nn.silu(blk @ w1) @ w2

def nsa_attention(q, k_cmp, v_cmp, k_slc, v_slc, k_win, v_win, gate_logit, rel_table,
                  pe_k, w1_k, w2_k, pe_v, w1_v, w2_v):
    B, T, H, DH = q.shape
    G, R = NSA_KV_GROUPS, NSA_REP
    nb = T // Q_BLOCK
    nc = (T - CMP_BLOCK) // CMP_STRIDE + 1
    ns = T // SLC_BLOCK
    n_sel = min(SLC_TOPK, ns)

    kc = compress_blocks(k_cmp, pe_k, w1_k, w2_k)
    vc = compress_blocks(v_cmp, pe_v, w1_v, w2_v)
    cmp_start = np.arange(nc) * CMP_STRIDE
    cmp_end = jnp.asarray(cmp_start + CMP_BLOCK - 1, dtype=jnp.int32)
    slc_start = np.arange(ns) * SLC_BLOCK
    overlap = jnp.asarray(((cmp_start[:, None] < slc_start[None, :] + SLC_BLOCK)
                           & (cmp_start[:, None] + CMP_BLOCK > slc_start[None, :])).astype(np.float32))

    tbl_heads = rel_table.T
    tbl_grp = tbl_heads.reshape(G, R, REL_BUCKETS)
    g_idx = jnp.arange(G)[None, :, None, None, None]
    r_idx = jnp.arange(R)[None, None, :, None, None]

    ks = k_slc.transpose(0, 2, 1, 3).reshape(B, G, ns, SLC_BLOCK, DH)
    vs = v_slc.transpose(0, 2, 1, 3).reshape(B, G, ns, SLC_BLOCK, DH)
    pad = ((0, 0), (0, 0), (WINDOW, 0), (0, 0))
    kwp = jnp.pad(k_win.transpose(0, 2, 1, 3), pad)
    vwp = jnp.pad(v_win.transpose(0, 2, 1, 3), pad)
    win_dist = jnp.asarray(np.arange(Q_BLOCK)[:, None] + WINDOW - np.arange(Q_BLOCK + WINDOW)[None, :],
                           dtype=jnp.int32)
    bias_win = tbl_heads[:, rel_bucket(win_dist)].reshape(G, R, Q_BLOCK, Q_BLOCK + WINDOW)

    qb = q.reshape(B, nb, Q_BLOCK, G, R, DH).transpose(1, 0, 3, 4, 2, 5)
    b_idx = jnp.arange(B)[:, None, None, None]
    gk_idx = jnp.arange(G)[None, :, None, None]
    j = jnp.arange(ns)

    def block(args):
        i, qi = args
        qpos = i * Q_BLOCK + jnp.arange(Q_BLOCK)
        s = jnp.einsum('bgrqd,bgcd->bgrqc', qi, kc).astype(jnp.float32) * SCALE
        bias = tbl_heads[:, rel_bucket(qpos[:, None] - cmp_end[None, :])].reshape(G, R, Q_BLOCK, nc)
        p_cmp = masked_softmax(s + bias, cmp_end[None, :] <= qpos[:, None])
        o_cmp = jnp.einsum('bgrqc,bgcd->bgrqd', p_cmp.astype(vc.dtype), vc)
        imp = jnp.einsum('bgrqc,cs->bgqs', p_cmp, overlap)
        cur = qpos // SLC_BLOCK
        forced = (j[None, :] == 0) | (j[None, :] == cur[:, None]) | (j[None, :] == cur[:, None] - 1)
        valid = j[None, :] * SLC_BLOCK <= qpos[:, None]
        imp = jnp.where(forced, FORCED_SCORE, jnp.where(valid, imp, -1.0))
        _, sel = lax.top_k(imp, n_sel)
        k_sel = ks[b_idx, gk_idx, sel].reshape(B, G, Q_BLOCK, n_sel * SLC_BLOCK, DH)
        v_sel = vs[b_idx, gk_idx, sel].reshape(B, G, Q_BLOCK, n_sel * SLC_BLOCK, DH)
        pos = (sel[..., None] * SLC_BLOCK + jnp.arange(SLC_BLOCK)).reshape(B, G, Q_BLOCK, n_sel * SLC_BLOCK)
        s = jnp.einsum('bgrqd,bgqkd->bgrqk', qi, k_sel).astype(jnp.float32) * SCALE
        bias = tbl_grp[g_idx, r_idx, rel_bucket(qpos[:, None] - pos)[:, :, None]]
        p = masked_softmax(s + bias, (pos <= qpos[:, None])[:, :, None])
        o_slc = jnp.einsum('bgrqk,bgqkd->bgrqd', p.astype(v_sel.dtype), v_sel)
        kw = lax.dynamic_slice_in_dim(kwp, i * Q_BLOCK, Q_BLOCK + WINDOW, axis=2)
        vw = lax.dynamic_slice_in_dim(vwp, i * Q_BLOCK, Q_BLOCK + WINDOW, axis=2)
        kpos = i * Q_BLOCK - WINDOW + jnp.arange(Q_BLOCK + WINDOW)
        wmask = ((kpos[None, :] >= 0) & (kpos[None, :] <= qpos[:, None])
                 & (qpos[:, None] - kpos[None, :] < WINDOW))
        s = jnp.einsum('bgrqd,bgkd->bgrqk', qi, kw).astype(jnp.float32) * SCALE + bias_win
        p = masked_softmax(s, wmask)
        o_win = jnp.einsum('bgrqk,bgkd->bgrqd', p.astype(vw.dtype), vw)
        return jnp.stack([o_cmp, o_slc, o_win], axis=-2)

    o = lax.map(block, (jnp.arange(nb), qb))
    o = o.transpose(1, 0, 4, 2, 3, 5, 6).reshape(B, T, H, 3, DH)
    gates = jax.nn.sigmoid(gate_logit)[..., None]
    return jnp.sum(gates * o, axis=3).reshape(B, T, H * DH)

def first_inputs(seed: int = 0) -> dict:
    key = jax.random.key(seed)
    ks = jax.random.split(key, 20)

    def w(k, shape, fan_in):
        return jax.random.normal(k, shape, jnp.float32) * fan_in ** -0.5

    def gain(k, shape):
        return 1.0 + 0.05 * jax.random.normal(k, shape, jnp.float32)

    nrm = lambda k, shape: jax.random.normal(k, shape, jnp.float32)
    L = DEPTH
    return {
        "x": nrm(ks[0], (BATCH, SEQ, D_MODEL)),
        "rel_bias_table": 0.5 * nrm(ks[1], (REL_BUCKETS, NSA_HEADS)),
        "g_attn": gain(ks[2], (L, D_MODEL)),
        "w_in": w(ks[3], (L, D_MODEL, IN_WIDTH), D_MODEL),
        "b_forget": 3.0 + 0.5 * nrm(ks[4], (L, FOX_HEADS)),
        "cmp_pe_k": 0.5 * nrm(ks[5], (L, CMP_BLOCK, HEAD_DIM)),
        "cmp_w1_k": w(ks[6], (L, CMP_BLOCK * HEAD_DIM, CMP_HIDDEN), CMP_BLOCK * HEAD_DIM),
        "cmp_w2_k": w(ks[7], (L, CMP_HIDDEN, HEAD_DIM), CMP_HIDDEN),
        "cmp_pe_v": 0.5 * nrm(ks[8], (L, CMP_BLOCK, HEAD_DIM)),
        "cmp_w1_v": w(ks[9], (L, CMP_BLOCK * HEAD_DIM, CMP_HIDDEN), CMP_BLOCK * HEAD_DIM),
        "cmp_w2_v": w(ks[10], (L, CMP_HIDDEN, HEAD_DIM), CMP_HIDDEN),
        "w_br_fox": w(ks[11], (L, FOX_W, D_MODEL), FOX_W),
        "w_br_nsa": w(ks[12], (L, NSA_W, D_MODEL), NSA_W),
        "w_out": w(ks[13], (L, D_MODEL, D_MODEL), D_MODEL),
        "g_mlp": gain(ks[14], (L, D_MODEL)),
        "w_ff1": w(ks[15], (L, D_MODEL, D_FF), D_MODEL),
        "w_ff2": w(ks[16], (L, D_FF, D_MODEL), D_FF),
        "g_final": gain(ks[17], (D_MODEL,)),
    }

def first_block(x, rel_bias_table, g_attn, w_in, b_forget, cmp_pe_k, cmp_w1_k, cmp_w2_k,
              cmp_pe_v, cmp_w1_v, cmp_w2_v, w_br_fox, w_br_nsa, w_out, g_mlp, w_ff1, w_ff2,
              g_final):
    B, T, _ = x.shape
    offsets = np.cumsum(IN_SPLITS)[:-1].tolist()
    for l in range(DEPTH):
        h = rms_norm(x, g_attn[l])
        z = h @ w_in[l]
        (fq, fk, fv, f_logit, nq, kc, vc, ksl, vsl, kwn, vwn, n_gate, g_a, g_b) = jnp.split(z, offsets, axis=-1)
        fox_h = lambda t: t.reshape(B, T, FOX_HEADS, HEAD_DIM)
        kv_h = lambda t: t.reshape(B, T, NSA_KV_GROUPS, HEAD_DIM)
        o_fox = fox_attention(fox_h(fq), fox_h(fk), fox_h(fv), f_logit, b_forget[l])
        o_nsa = nsa_attention(nq.reshape(B, T, NSA_HEADS, HEAD_DIM), kv_h(kc), kv_h(vc), kv_h(ksl), kv_h(vsl),
                              kv_h(kwn), kv_h(vwn), n_gate.reshape(B, T, NSA_HEADS, 3), rel_bias_table,
                              cmp_pe_k[l], cmp_w1_k[l], cmp_w2_k[l], cmp_pe_v[l], cmp_w1_v[l], cmp_w2_v[l])
        merged = jax.nn.sigmoid(g_a) * (o_fox @ w_br_fox[l]) + jax.nn.sigmoid(g_b) * (o_nsa @ w_br_nsa[l])
        x = x + merged @ w_out[l]
        h = rms_norm(x, g_mlp[l])
        x = x + jnp.square(jax.nn.relu(h @ w_ff1[l])) @ w_ff2[l]
    return rms_norm(x, g_final)


N_META = 16
BLOCK = 128
PAD = BLOCK - N_META
WINDOW_2 = 128
A_HEADS = 8
A_KV_HEADS = 2
A_HEAD_DIM = 64
B_HEADS = 8
B_HEAD_DIM = 64
B_Q_RANK = 256
B_KV_RANK = 128
IDX_HEADS = 4
IDX_DIM = 64
TOPK_MAX = 256
N_BUCKETS = 32
MAX_DISTANCE = 128
TOTAL_HEADS = A_HEADS + B_HEADS
D_FF_2 = -(-8 * D_MODEL // (3 * 256)) * 256
EPS = 1e-6
NEG = -1e30

IN_WIDTHS = (A_HEADS * A_HEAD_DIM, A_KV_HEADS * A_HEAD_DIM, A_KV_HEADS * A_HEAD_DIM,
             B_Q_RANK, B_KV_RANK, IDX_HEADS * IDX_DIM, IDX_DIM, IDX_HEADS, 2 * D_MODEL)
IN_SPLITS_2 = tuple(sum(IN_WIDTHS[:i + 1]) for i in range(len(IN_WIDTHS) - 1))
D_IN = sum(IN_WIDTHS)


def rms_norm_2(x, g):
    xf = x.astype(jnp.float32)
    y = xf * lax.rsqrt(jnp.mean(xf * xf, axis=-1, keepdims=True) + EPS)
    return (y * g.astype(jnp.float32)).astype(x.dtype)

def layer_norm(x, g, b):
    xf = x.astype(jnp.float32)
    mu = jnp.mean(xf, axis=-1, keepdims=True)
    xc = xf - mu
    var = jnp.mean(xc * xc, axis=-1, keepdims=True)
    return (xc * lax.rsqrt(var + EPS) * g.astype(jnp.float32) + b.astype(jnp.float32)).astype(x.dtype)

def t5_bucket(dist):
    max_exact = N_BUCKETS // 2
    d = jnp.maximum(dist, 1).astype(jnp.float32)
    large = max_exact + (jnp.log(d / max_exact) / math.log(MAX_DISTANCE / max_exact)
                         * (N_BUCKETS - max_exact)).astype(jnp.int32)
    large = jnp.minimum(large, N_BUCKETS - 1)
    return jnp.where(dist < max_exact, dist, large)

def sliding_window_sink_attention(q, k, v, sinks, bias_table):
    b, p, _ = q.shape
    nb = p // BLOCK
    grp = A_HEADS // A_KV_HEADS
    qb = q.reshape(b, nb, BLOCK, A_KV_HEADS, grp, A_HEAD_DIM)
    kb = k.reshape(b, nb, BLOCK, A_KV_HEADS, A_HEAD_DIM)
    vb = v.reshape(b, nb, BLOCK, A_KV_HEADS, A_HEAD_DIM)

    def with_prev(t):
        prev = jnp.concatenate([jnp.zeros_like(t[:, :1]), t[:, :-1]], axis=1)
        return jnp.concatenate([prev, t], axis=2)

    kw, vw = with_prev(kb), with_prev(vb)
    s = jnp.einsum('bnqhgd,bnkhd->bnhgqk', qb, kw).astype(jnp.float32) * (A_HEAD_DIM ** -0.5)
    blk = jnp.arange(nb)[:, None] * BLOCK
    qpos = blk + jnp.arange(BLOCK)[None]
    kpos = blk - BLOCK + jnp.arange(2 * BLOCK)[None]
    dist = qpos[:, :, None] - kpos[:, None, :]
    allowed = (dist >= 0) & (dist < WINDOW_2) & (kpos[:, None, :] >= PAD)
    bias = bias_table[t5_bucket(jnp.maximum(dist, 0))]
    bias = bias.reshape(nb, BLOCK, 2 * BLOCK, A_KV_HEADS, grp).transpose(0, 3, 4, 1, 2)
    s = jnp.where(allowed[None, :, None, None], s + bias.astype(jnp.float32)[None], NEG)
    sink = sinks.astype(jnp.float32).reshape(A_KV_HEADS, grp)[None, None, :, :, None]
    m = jnp.maximum(s.max(axis=-1), sink)
    e = jnp.exp(s - m[..., None])
    pr = e / (e.sum(axis=-1, keepdims=True) + jnp.exp(sink - m)[..., None])
    o = jnp.einsum('bnhgqk,bnkhd->bnqhgd', pr.astype(v.dtype), vw)
    return o.reshape(b, p, A_HEADS * A_HEAD_DIM)

def indexed_sparse_mla(q_abs, c_kv, iq, ik, iw, w_uv, bias_table):
    b, p, _, _ = q_abs.shape
    nb = p // BLOCK
    topk = min(TOPK_MAX, (p - BLOCK) // 4)
    kpos = jnp.arange(p)
    gather = jax.vmap(lambda rows, idx: rows[idx])
    scale = B_HEAD_DIM ** -0.5

    def one_block(i):
        start = i * BLOCK
        qa = lax.dynamic_slice_in_dim(q_abs, start, BLOCK, axis=1)
        qi = lax.dynamic_slice_in_dim(iq, start, BLOCK, axis=1)
        wi = lax.dynamic_slice_in_dim(iw, start, BLOCK, axis=1)
        qpos = start + jnp.arange(BLOCK)
        logits = jnp.einsum('bqhd,bsd->bqhs', qi, ik)
        score = jnp.einsum('bqhs,bqh->bqs', jax.nn.relu(logits).astype(jnp.float32),
                           wi.astype(jnp.float32))
        admissible = (kpos[None, :] <= qpos[:, None]) & (kpos[None, :] >= PAD)
        score = jnp.where(admissible[None], score, -jnp.inf)
        _, sel = lax.top_k(score, topk)
        valid = (sel <= qpos[None, :, None]) & (sel >= PAD)
        c_sel = gather(c_kv, sel)
        s = jnp.einsum('bqhc,bqkc->bqhk', qa, c_sel).astype(jnp.float32) * scale
        bias = bias_table[t5_bucket(jnp.maximum(qpos[None, :, None] - sel, 0))]
        s = jnp.where(valid[:, :, None, :], s + jnp.moveaxis(bias, -1, 2).astype(jnp.float32), NEG)
        pr = jax.nn.softmax(s, axis=-1)
        return jnp.einsum('bqhk,bqkc->bqhc', pr.astype(c_kv.dtype), c_sel)

    lat = lax.map(one_block, jnp.arange(nb))
    lat = lat.transpose(1, 0, 2, 3, 4).reshape(b, p, B_HEADS, B_KV_RANK)
    o = jnp.einsum('bphc,chd->bphd', lat, w_uv)
    return o.reshape(b, p, B_HEADS * B_HEAD_DIM)

def second_inputs(seed: int = 0) -> dict:
    key = jax.random.key(seed)
    ks = jax.random.split(key, 24)
    f32 = jnp.float32

    def dense(k, shape, fan_in):
        return jax.random.normal(k, shape, f32) * (fan_in ** -0.5)

    def gain(k, shape):
        return 1.0 + 0.05 * jax.random.normal(k, shape, f32)

    return {
        "x": jax.random.normal(ks[0], (BATCH, SEQ, D_MODEL), f32),
        "meta_tokens": jax.random.normal(ks[1], (N_META, D_MODEL), f32),
        "attn_norm_g": gain(ks[2], (DEPTH, D_MODEL)),
        "w_in": dense(ks[3], (DEPTH, D_MODEL, D_IN), D_MODEL),
        "b_gates": 0.02 * jax.random.normal(ks[4], (DEPTH, 2 * D_MODEL), f32),
        "q_norm_g": gain(ks[5], (DEPTH, B_Q_RANK)),
        "kv_norm_g": gain(ks[6], (DEPTH, B_KV_RANK)),
        "w_uq": dense(ks[7], (DEPTH, B_Q_RANK, B_HEADS * B_HEAD_DIM), B_Q_RANK),
        "w_uk": dense(ks[8], (DEPTH, B_KV_RANK, B_HEADS, B_HEAD_DIM), B_KV_RANK),
        "w_uv": dense(ks[9], (DEPTH, B_KV_RANK, B_HEADS, B_HEAD_DIM), B_KV_RANK),
        "idx_k_ln_g": gain(ks[10], (DEPTH, IDX_DIM)),
        "idx_k_ln_b": 0.02 * jax.random.normal(ks[11], (DEPTH, IDX_DIM), f32),
        "sinks": 0.5 * jax.random.normal(ks[12], (DEPTH, A_HEADS), f32),
        "rel_bias": 0.2 * jax.random.normal(ks[13], (N_BUCKETS, TOTAL_HEADS), f32),
        "w_branch_a": dense(ks[14], (DEPTH, A_HEADS * A_HEAD_DIM, D_MODEL), A_HEADS * A_HEAD_DIM),
        "w_branch_b": dense(ks[15], (DEPTH, B_HEADS * B_HEAD_DIM, D_MODEL), B_HEADS * B_HEAD_DIM),
        "w_out": dense(ks[16], (DEPTH, D_MODEL, D_MODEL), D_MODEL),
        "ffn_norm_g": gain(ks[17], (DEPTH, D_MODEL)),
        "w_ffn_gate": dense(ks[18], (DEPTH, D_MODEL, D_FF_2), D_MODEL),
        "w_ffn_up": dense(ks[19], (DEPTH, D_MODEL, D_FF_2), D_MODEL),
        "w_ffn_down": dense(ks[20], (DEPTH, D_FF_2, D_MODEL), D_FF_2),
        "final_norm_g": gain(ks[21], (D_MODEL,)),
    }

def second_block(x, meta_tokens, attn_norm_g, w_in, b_gates, q_norm_g, kv_norm_g, w_uq, w_uk, w_uv,
              idx_k_ln_g, idx_k_ln_b, sinks, rel_bias, w_branch_a, w_branch_b, w_out,
              ffn_norm_g, w_ffn_gate, w_ffn_up, w_ffn_down, final_norm_g):
    b, seq, d = x.shape
    meta = jnp.broadcast_to(meta_tokens.astype(x.dtype)[None], (b, N_META, d))
    h = jnp.concatenate([jnp.zeros((b, PAD, d), x.dtype), meta, x], axis=1)
    p = h.shape[1]
    bias_a = rel_bias[:, :A_HEADS]
    bias_b = rel_bias[:, A_HEADS:]
    for l in range(DEPTH):
        hn = rms_norm_2(h, attn_norm_g[l])
        proj = hn @ w_in[l]
        aq, ak, av, bq, bkv, iq, ik, iw, gates = jnp.split(proj, IN_SPLITS_2, axis=-1)
        gates = jax.nn.sigmoid((gates + b_gates[l]).astype(jnp.float32)).astype(h.dtype)
        gate_a, gate_b = jnp.split(gates, 2, axis=-1)
        o_a = sliding_window_sink_attention(aq, ak, av, sinks[l], bias_a)
        q = (rms_norm_2(bq, q_norm_g[l]) @ w_uq[l]).reshape(b, p, B_HEADS, B_HEAD_DIM)
        c_kv = rms_norm_2(bkv, kv_norm_g[l])
        q_abs = jnp.einsum('bphd,chd->bphc', q, w_uk[l])
        iq = iq.reshape(b, p, IDX_HEADS, IDX_DIM)
        ik = layer_norm(ik, idx_k_ln_g[l], idx_k_ln_b[l])
        iw = iw * ((IDX_HEADS * IDX_DIM) ** -0.5)
        o_b = indexed_sparse_mla(q_abs, c_kv, iq, ik, iw, w_uv[l], bias_b)
        mixed = gate_a * (o_a @ w_branch_a[l]) + gate_b * (o_b @ w_branch_b[l])
        h = h + mixed @ w_out[l]
        hn = rms_norm_2(h, ffn_norm_g[l])
        h = h + (jax.nn.silu(hn @ w_ffn_gate[l]) * (hn @ w_ffn_up[l])) @ w_ffn_down[l]
    y = rms_norm_2(h, final_norm_g)
    return y[:, PAD + N_META:]


def setup_inputs(seed=0):
    out = dict(first_inputs(seed))
    for name, value in second_inputs(seed + 1).items():
        if name != "x":
            out[name + "_2"] = value
    return out


def reference(
    x, rel_bias_table, g_attn, w_in, b_forget, cmp_pe_k, cmp_w1_k, cmp_w2_k, cmp_pe_v, cmp_w1_v,
    cmp_w2_v, w_br_fox, w_br_nsa, w_out, g_mlp, w_ff1, w_ff2, g_final, meta_tokens_2,
    attn_norm_g_2, w_in_2, b_gates_2, q_norm_g_2, kv_norm_g_2, w_uq_2, w_uk_2, w_uv_2,
    idx_k_ln_g_2, idx_k_ln_b_2, sinks_2, rel_bias_2, w_branch_a_2, w_branch_b_2, w_out_2,
    ffn_norm_g_2, w_ffn_gate_2, w_ffn_up_2, w_ffn_down_2, final_norm_g_2,
):
    x = first_block(
        x, rel_bias_table, g_attn, w_in, b_forget, cmp_pe_k, cmp_w1_k, cmp_w2_k, cmp_pe_v,
        cmp_w1_v, cmp_w2_v, w_br_fox, w_br_nsa, w_out, g_mlp, w_ff1, w_ff2, g_final,
    )
    return second_block(
        x, meta_tokens_2, attn_norm_g_2, w_in_2, b_gates_2, q_norm_g_2, kv_norm_g_2, w_uq_2,
        w_uk_2, w_uv_2, idx_k_ln_g_2, idx_k_ln_b_2, sinks_2, rel_bias_2, w_branch_a_2,
        w_branch_b_2, w_out_2, ffn_norm_g_2, w_ffn_gate_2, w_ffn_up_2, w_ffn_down_2,
        final_norm_g_2,
    )


_drawn_inputs = setup_inputs


def setup_inputs(seed=0):
    import zlib

    import numpy as np

    out = dict(_drawn_inputs(seed))
    spreads = {}
    factors = {'cmp_pe_k': 4.62,
     'b_gates_2': 8.0,
     'q_norm_g_2': 8.0,
     'kv_norm_g_2': 4.542,
     'idx_k_ln_g_2': 4.916,
     'idx_k_ln_b_2': 8.0,
     'sinks_2': 29.869,
     'rel_bias_2': 2.739,
     'ffn_norm_g_2': 3.489}
    for name, (base, spread) in spreads.items():
        noise = np.random.default_rng([zlib.crc32(name.encode()), seed]).standard_normal(out[name].shape)
        drawn = base * np.exp(spread * noise) if base else spread * noise
        out[name] = jnp.asarray(drawn.astype(out[name].dtype))
    for name, factor in factors.items():
        out[name] = (out[name] * factor).astype(out[name].dtype)
    return out
```

```python
from contextlib import ExitStack

import numpy as np

import concourse.bass as bass
from concourse import mybir

F = mybir.dt.float32
R = mybir.dt.float32r
BF = mybir.dt.bfloat16
ALU = mybir.AluOpType
ACT = mybir.ActivationFunctionType
AX = mybir.AxisListType

T = 512
NM = 16
TM = T + NM
D = 1024
H = 8
HD = 64
NC = 31
RAW = 4
SPL = 3
NEG = -1e30
NADM = -1e37
NREP = -3e38
EPS = 1e-6
NOH = 1024
NR_ = 672
SIZES2 = (8, 8, 6)


def tile_list():
    t = []
    t += [("fq", i, 1024, True) for i in range(4)]
    t += [("fk", i, 1024, True) for i in range(4)]
    t += [("fv", i, 1024, True) for i in range(4)]
    t += [("a2", i, 288 * n, True) for i, n in enumerate((3, 3, 2))]
    t += [("nq", i, 1024, True) for i in range(4)]
    t += [("kv", i, 1024, True) for i in range(4)]
    t += [("w1k", i, 1024, False) for i in range(4)]
    t += [("w1v", i, 1024, False) for i in range(4)]
    for i in range(8):
        t += [("ga", i, 1024, True), ("gb", i, 1024, True), ("br", i, 1024, True)]
    t += [("wo", i, 1024, True) for i in range(8)]
    for q in range(4):
        t += [("f1", 8 * q + i, 1024, True) for i in range(8)]
        t += [("f2", 8 * q + i, 1024, True) for i in range(8)]
    t += [("ik", i, 196 * n, True) for i, n in enumerate((5, 3))]
    t += [("iq", i, 1024, True) for i in range(2)]
    t += [("bkv", 0, 1024, True)]
    t += [("bq", i, 1024, True) for i in range(2)]
    t += [("ak", 0, 1024, True)]
    t += [("aq", i, 1024, True) for i in range(4)]
    t += [("uq", 0, 1024, True), ("ukv", 0, 1024, True)]
    for i in range(8):
        t += [("ga2", i, 1024, True), ("gb2", i, 1024, True), ("br2", i, 1024, True)]
    t += [("wo2", i, 1024, True) for i in range(8)]
    f = 0
    for c, n in enumerate(SIZES2):
        for i in range(n):
            t += [("fg", f + i, 1024, True), ("fu", f + i, 1024, True)]
        t += [("fd", 8 * c + i, n * 128, True) for i in range(8)]
        f += n
    return t


def C(fn, *args, **kw):
    return lambda: fn(*args, **kw)


def build(nc, d, out):
    tiles = tile_list()
    with ExitStack() as ctx:
        def sb(name, shape, dt=F):
            return ctx.enter_context(nc.sbuf_tensor(name, shape, dt))

        def sem(name):
            return ctx.enter_context(nc.semaphore(name))

        nds = [0]

        class Queue:

            def __init__(self, name, eng):
                self.eng, self.sem, self.n, self.q, self.seen = eng, sem(name), 0, [], {}

            def wait(self, *toks):
                for tok in toks:
                    if tok is None:
                        continue
                    if isinstance(tok, list):
                        self.wait(*tok)
                        continue
                    s, v = tok
                    if self.seen.get(id(s), 0) < v:
                        self.seen[id(s)] = v
                        self.q.append(lambda s=s, v=v: self.eng.wait_ge(s, v))

            def op(self, fn, *toks, inc=True):
                self.wait(*toks)
                if not inc:
                    self.q.append(fn)
                    return None
                self.n += 1
                self.q.append(lambda: fn().then_inc(self.sem, 1))
                return (self.sem, self.n)

            def dma(self, dst, src, ds, *toks):
                self.wait(*toks)
                if ds is None:
                    nds[0] += 1
                    ds = [sem(f"s_dma{nds[0]}"), 0]
                self.q.append(lambda: self.eng.dma_start(dst, src).then_inc(ds[0], 16))
                ds[1] += 16
                return (ds[0], ds[1])

        PE = Queue("s_pe", nc.tensor)
        DV = Queue("s_dv", nc.vector)
        AC = Queue("s_ac", nc.scalar)
        PL = Queue("s_pl", nc.gpsimd)
        SP = Queue("s_sp", nc.sync)
        pe, dv, ac, pl = nc.tensor, nc.vector, nc.scalar, nc.gpsimd

        def dsem(name):
            return [sem(name), 0]

        Ah, Al = sb("Ah", [128, 8, TM], R), sb("Al", [128, 8, TM], R)
        Bh, Bl = sb("Bh", [128, 8, T], R), sb("Bl", [128, 8, T], R)
        WH = [sb(f"WH{i}", [128, 1024], R) for i in range(SPL)]
        WL = [sb(f"WL{i}", [128, 1024], R) for i in range(SPL)]
        WR = [sb(f"WR{i}", [128, 1024]) for i in range(RAW)]
        XT = sb("XT", [128, 8 * TM])
        AR = sb("AR", [128, 20288])
        CTX = sb("CTX", [128, 2 * T])
        CS2 = sb("CS2", [128, 416])
        CST = sb("CST", [128, 196])
        ONE = sb("ONE", [128, 1])
        IDB = sb("IDB", [128, 128], BF)
        PSA = ctx.enter_context(nc.psum_tensor("PSA", [128, 8, 512], F))
        PSF = PSA[:, :, :].rearrange("p b c -> p (b c)")

        def bank(i):
            return PSA[:, i, :]

        ident, ones = CST[:, 0:128], ONE[:, 0:1].to_broadcast([128, 128])
        gv = [CST[:, 128 + 8 * i:136 + 8 * i] for i in range(6)]
        one_h = CST[0:8, 178:186]
        bfor = CST[0:8, 186:187]
        vals = CST[:, 187:191]
        qn = CST[:, 192:194]
        kvn = CST[:, 194:195]

        c_tok = SP.dma(CST[:, :], d["cst"], None)
        c2_tok = PL.dma(CS2[:, 0:416], d["cs1"], None)
        one_tok = DV.op(C(dv.memset, ONE[:, :], 1.0))
        idb_tok = DV.op(C(dv.tensor_copy, IDB[:, :], ident), c_tok)
        x3 = XT[:, :].rearrange("p (k t) -> p k t", k=8)
        x_tok = SP.dma(x3[:, :, 0:T], d["xT"], None)

        raw_sem = [dsem(f"s_raw{i}") for i in range(RAW)]
        raw_free = [None] * RAW
        split_free = [None] * SPL
        loaded, ready = {}, {}
        st = {"dma": 0, "split": 0, "use": 0, "ns": 0}

        def load_tile():
            j = st["dma"]
            if j >= len(tiles):
                return
            st["dma"] += 1
            s, n = j % RAW, tiles[j][2]
            loaded[j] = SP.dma(WR[s][:, 0:n], d["w"][j, :, 0:n], raw_sem[s], raw_free[s])

        for _ in range(RAW):
            load_tile()

        def split_tile():
            j = st["split"]
            if j >= len(tiles):
                return
            st["split"] += 1
            name, _, n, split = tiles[j]
            s = j % RAW
            if not split:
                ready[j] = ([loaded[j]], WR[s], None)
                return
            p = st["ns"] % SPL
            st["ns"] += 1
            hi = AC.op(C(ac.copy, WH[p][:, 0:n], WR[s][:, 0:n]), loaded[j], split_free[p])
            lo = DV.op(C(dv.tensor_tensor, WL[p][:, 0:n], WR[s][:, 0:n], WH[p][:, 0:n].bitcast(F), ALU.subtract),
                       hi, loaded[j], split_free[p])
            raw_free[s] = [hi, lo]
            ready[j] = ([hi, lo], p, None)
            load_tile()

        def next_tile(name):
            j = st["use"]
            assert tiles[j][0] == name, (tiles[j], name)
            st["use"] += 1
            while st["split"] <= j + (SPL - 1 if tiles[j][3] else 0) and st["split"] < len(tiles):
                if st["split"] > j and not (tiles[st["split"]][3] and tiles[j][3]):
                    break
                split_tile()
            PE.wait(ready[j][0])
            return j, ready[j][1]

        def tile_done(j, tok):
            if tiles[j][3]:
                split_free[ready[j][1]] = tok
            else:
                raw_free[j % RAW] = tok
                load_tile()

        def mm(o, l, r, start, stop, *toks, inc=False):
            return PE.op(C(pe.matmul, o, l, r, start=start, stop=stop), *toks, inc=inc)

        def feat(name, src, nk, o, *toks, kmap=None, ncol=T, cols=None, om=None, skip0=0):
            j, p = next_tile(name)
            PE.wait(*toks)
            w = cols or (lambda W, k: W[:, k * 128:(k + 1) * 128])
            sh, sl = src
            for k in range(nk):
                PE.wait(kmap[k] if kmap else None)
                a, b = w(WH[p], k), w(WL[p], k)
                s0, e = k == 0, k == nk - 1
                mm(o, a, sh(k, 0, T), s0, False)
                mm(o, a, sl(k, 0, T), False, False)
                last = mm(o, b, sh(k, 0, T), False, e, inc=e)
            if om is not None:
                for k in range(nk):
                    a, b = w(WH[p], k), w(WL[p], k)
                    s0, e = k == 0, k == nk - 1
                    mm(om, a, sh(k, T, TM), s0, False)
                    mm(om, a, sl(k, T, TM), False, False)
                    last = mm(om, b, sh(k, T, TM), False, e, inc=e)
            tile_done(j, last)
            return last

        hA = (lambda k, a, b: Ah[:, k, a:b], lambda k, a, b: Al[:, k, a:b])
        hB = (lambda k, a, b: Bh[:, k, a:b], lambda k, a, b: Bl[:, k, a:b])

        def barrier():
            toks = [(e.sem, e.n) for e in (PE, DV, AC, PL) if e.n]
            for e in (PE, DV, AC, PL):
                e.wait(*toks)
            return toks

        free = [None] * 8

        def rms(X, nk, width, n, gcol, put, xtok, tmp, b0, b1, dst=None):
            sq = [tmp[:, 0:TM], tmp[:, TM:2 * TM]]
            sqf = [None, None]
            st_tok = None
            for k in range(nk):
                a = AC.op(C(ac.activation, sq[k % 2][:, 0:width], X(k), ACT.Square),
                          xtok(k), sqf[k % 2])
                last = mm(bank(b0)[:, 0:min(width, T)], ones, sq[k % 2][:, 0:min(width, T)], k == 0, k == nk - 1,
                          a, free[b0], one_tok, inc=True)
                if width > T:
                    last = mm(bank(b1)[:, 0:width - T], ones, sq[k % 2][:, T:width], k == 0, k == nk - 1,
                              free[b1], inc=True)
                sqf[k % 2] = last
            v, r, u = tmp[:, 2 * TM:3 * TM], tmp[:, 3 * TM:4 * TM], tmp[:, 4 * TM:5 * TM]
            pieces = [(b0, 0, min(width, T))] + ([(b1, T, width)] if width > T else [])
            for b, lo, hi in pieces:
                st_tok = DV.op(C(dv.tensor_scalar, 
                    v[:, lo:hi], bank(b)[:, 0:hi - lo], 1.0 / n, EPS, ALU.mult, ALU.add), last)
                free[b] = st_tok
            W = slice(0, width)
            t1 = AC.op(C(ac.activation, r[:, W], v[:, W], ACT.Ln), st_tok)
            t1 = AC.op(C(ac.activation, r[:, W], r[:, W], ACT.Exp, scale=-0.5), t1)
            t2 = DV.op(C(dv.tensor_tensor, u[:, W], r[:, W], r[:, W], ALU.mult), t1)
            t2 = DV.op(C(dv.scalar_tensor_tensor, out=u[:, W], in0=u[:, W], scalar=-0.5, in1=v[:, W],
                                                       op0=ALU.mult, op1=ALU.mult), t2)
            t2 = DV.op(C(dv.scalar_tensor_tensor, out=r[:, W], in0=u[:, W], scalar=1.5, in1=r[:, W],
                                                       op0=ALU.add, op1=ALU.mult), t2)
            hb = [tmp[:, 5 * TM:6 * TM], tmp[:, 6 * TM:7 * TM]]
            hf = [None, None]
            for k in range(nk):
                t = DV.op(C(dv.scalar_tensor_tensor, 
                    out=dst(k) if dst else hb[k % 2][:, W], in0=X(k), scalar=gcol[:, k:k + 1], in1=r[:, W],
                    op0=ALU.mult, op1=ALU.mult), t2, hf[k % 2], c_tok, xtok(k))
                hf[k % 2] = put(k, hb[k % 2][:, W], t)
            return hf

        def split_to(hi, lo, src, tok, *toks):
            a = AC.op(C(ac.copy, hi, src), tok, *toks)
            b = DV.op(C(dv.tensor_tensor, lo, src, hi.bitcast(F), ALU.subtract), a)
            return [a, b]

        hk = {}

        def norm_to_A(width, gcol, xtok, *waits):
            AC.wait(*waits)
            DV.wait(*waits)

            def put(k, src, t):
                hk[k] = split_to(Ah[:, k, 0:width], Al[:, k, 0:width], src, t)
                return hk[k]

            tmp = AR[:, 0:7 * TM]
            rms(lambda k: x3[:, k, 0:width], 8, width, float(D), gcol, put, xtok, tmp, 0, 1)
            return [hk[7][0], hk[7][1]]

        def evac(o, i, scale, tok, *toks, eng=None):
            if eng is AC:
                return AC.op(C(ac.activation, o, i, ACT.Copy, scale=scale), tok, *toks)
            return DV.op(C(dv.tensor_scalar, o, i, scale, None, ALU.mult), tok, *toks)

        done = norm_to_A(T, gv[0], lambda k: [x_tok, c_tok])

        FQ, FK = AR[:, 0:2048].rearrange("p (a t) -> p a t", a=4), AR[:, 2048:4096].rearrange("p (a t) -> p a t", a=4)
        FV = AR[:, 4096:6144].rearrange("p (a t) -> p a t", a=4)
        XKV = [AR[:, 6144 + 1024 * i:7168 + 1024 * i].rearrange("p (g t) -> p g t", g=2) for i in range(2)]
        NQ = AR[:, 8192:10240].rearrange("p (a t) -> p a t", a=4)
        KS = AR[:, 10240:11264].rearrange("p (g t) -> p g t", g=2)
        KW = AR[:, 11264:12288].rearrange("p (g t) -> p g t", g=2)
        V2 = AR[:, 12288:13312].rearrange("p (a t) -> p a t", a=4)
        FG = AR[:, 13312:13440].rearrange("p (a t) -> p a t", a=4)
        BC = AR[:, 13440:14432].rearrange("p (a h n) -> p a h n", a=4, h=H)
        MK = AR[:, 14432:14944]
        EB = [AR[:, 14944 + 528 * i:15472 + 528 * i] for i in range(2)]
        PB = [AR[:, 16000 + 528 * i:16528 + 528 * i] for i in range(2)]
        PTB = [AR[:, 17056 + 640 * i:17696 + 640 * i] for i in range(2)]
        OB = [AR[:, 18336 + 512 * i:18848 + 512 * i] for i in range(2)]
        OT = AR[:, 19360:19872]
        SM = AR[:, 19872:20288]
        nmx = [SM[:, 8 * i:8 * i + 8] for i in range(4)]
        rsm = [SM[:, 32 + 8 * i:40 + 8 * i] for i in range(4)]
        rcp = [SM[:, 64 + 8 * i:72 + 8 * i] for i in range(4)]
        GT = SM[:, 96:192].rearrange("p (a h b) -> p a h b", a=4, h=H)
        BFX = XT[:, 0:4096].rearrange("p (h t) -> p h t", h=H)

        OHF = AR[0:34, 14944:14944 + NOH]
        OHR = AR[0:34, 15968:15968 + NR_]
        TB = AR[0:34, 16992:17016]
        GR = AR[0:24, 17056:17056 + NR_]
        o_tok = [PL.dma(OHF, d["ohf"], None), PL.dma(OHR, d["ohr"], None), PL.dma(TB, d["tab"], None)]
        m_tok = PL.dma(MK, d["mk"], None)
        for c in range(2):
            last = mm(bank(4 + c)[0:24, 0:336], TB, OHR[:, 336 * c:336 * c + 336], True, True, o_tok, inc=True)
        gt = None
        for c in range(2):
            gt = DV.op(C(dv.tensor_copy, GR[:, 336 * c:336 * c + 336], bank(4 + c)[0:24, 0:336]), last)
            free[4 + c] = gt
        g_tok = PL.dma(d["scr"], GR[:, :].rearrange("p (u m) -> p u m", u=1).to_broadcast([24, 16, NR_]), None, gt)
        for a in range(4):
            for n in range(NC):
                off = 128 * a - 16 * n - 31 + 511
                b = 6 + a // 2
                o = bank(b)[:, (a % 2) * 256 + 8 * n:(a % 2) * 256 + 8 * n + 8]
                lt = mm(o, OHF[:, off:off + 128], TB[:, 0:8], True, True, inc=(a % 2 == 1 and n == NC - 1))
                last = lt or last
            if a % 2 == 1:
                for aa in (a - 1, a):
                    bc_tok = DV.op(C(dv.tensor_copy, 
                        BC[:, aa, :, :], bank(b)[:, (aa % 2) * 256:(aa % 2) * 256 + 248].rearrange(
                            "p (n h) -> p h n", h=H)), last)
                free[b] = bc_tok

        def toep(dst, c0, base, width, *toks):
            tk = []
            for a in range(8):
                src = bass.AP(tensor=d["scr"].tensor, offset=c0 * 16 * NR_ + base - 16 * a,
                              ap=[[NR_ - 1, 16], [16 * NR_, H], [1, width]])
                tk.append(PL.dma(dst[16 * a:16 * a + 16, :, :], src, None, *toks))
            return tk

        bf_tok = toep(BFX, 0, 143, T, g_tok, done)
        arena_tok = [done, last, gt, g_tok]

        AC.wait(done)
        DV.wait(done)
        nb = [0]

        def pb():
            nb[0] += 1
            return nb[0] % 2

        kc0 = dict(hk)
        for i in range(4):
            b = pb()
            t = feat("fq", hA, 8, bank(b), free[b], kmap=kc0)
            free[b] = fq_tok = evac(FQ[:, i, :], bank(b), 0.125, t, eng=AC)
        for i in range(4):
            b = pb()
            t = feat("fk", hA, 8, bank(b), free[b])
            free[b] = fk_tok = evac(FK[:, i, :], bank(b), 1.0, t)

        def tokmajor(name, widths, n, ks, mt=False, banks=(0, 1, 2, 3), mbank=None):
            k = 0
            for q, cnt in enumerate(ks):
                j, p = next_tile(name)
                for a in range(4):
                    PE.wait(free[banks[a]])
                    for kk in range(cnt):
                        kx = k + kk
                        PE.wait(hk[kx])
                        s0, e = kx == 0, kx == 7
                        wa, wb = WH[p][:, kk * n:(kk + 1) * n], WL[p][:, kk * n:(kk + 1) * n]
                        h1, l1 = Ah[:, kx, 128 * a:128 * a + 128], Al[:, kx, 128 * a:128 * a + 128]
                        mm(bank(banks[a])[:, 0:n], h1, wa, s0, False)
                        mm(bank(banks[a])[:, 0:n], l1, wa, False, False)
                        last = mm(bank(banks[a])[:, 0:n], h1, wb, False, e, inc=kk == cnt - 1)
                if mt:
                    PE.wait(free[mbank])
                    for kk in range(cnt):
                        kx = k + kk
                        PE.wait(hk[kx])
                        s0, e = kx == 0, kx == 7
                        wa, wb = WH[p][:, kk * n:(kk + 1) * n], WL[p][:, kk * n:(kk + 1) * n]
                        h1, l1 = Ah[:, kx, T:TM], Al[:, kx, T:TM]
                        mm(bank(mbank)[0:NM, 0:n], h1, wa, s0, False)
                        mm(bank(mbank)[0:NM, 0:n], l1, wa, False, False)
                        last = mm(bank(mbank)[0:NM, 0:n], h1, wb, False, e, inc=kk == cnt - 1)
                tile_done(j, last)
                k += cnt
            return last

        t = tokmajor("fv", None, 512, (2, 2, 2, 2))
        for a in range(4):
            free[a] = fv_tok = evac(FV[:, a, :], bank(a), 1.0, t, eng=AC if a % 2 else DV)
        fv_toks = [free[2], free[3]]
        t = tokmajor("a2", None, 288, (3, 3, 2))
        for a in range(4):
            t1 = evac(V2[:, a, :], bank(a)[:, 0:256], 1.0, t)
            free[a] = fg_tok = DV.op(C(dv.tensor_copy, FG[:, a, :], bank(a)[:, 256:288]), t)
        v2_tok = fg_tok
        LF = OB[0][0:8, :]
        LT = OB[1][0:8, :]
        for a in range(4):
            last = PE.op(C(pe.transpose, bank(4)[0:8, 128 * a:128 * a + 128], FG[:, a, 0:8], ident),
                         fg_tok, free[4], c_tok)
        t1 = DV.op(C(dv.tensor_scalar, LF, bank(4)[0:8, :], bfor, None, ALU.add), last, arena_tok)
        free[4] = t1
        t2 = DV.op(C(dv.scalar_tensor_tensor, out=LT, in0=LF, scalar=-1.0, in1=LF, op0=ALU.mult, op1=ALU.max), t1)
        t3 = AC.op(C(ac.activation, LT, LT, ACT.Exp, scale=-1.0), t2)
        t3 = AC.op(C(ac.activation, LT, LT, ACT.Ln, bias=1.0), t3)
        t4 = DV.op(C(dv.scalar_tensor_tensor, out=LF, in0=LF, scalar=0.0, in1=LT, op0=ALU.min,
                                                   op1=ALU.subtract), t3)
        t4 = DV.op(C(dv.memset, LT, 1.0), t4)
        ct_tok = DV.op(C(dv.tensor_tensor_scan, CTX[0:8, 0:T], LT, LF, 0.0, ALU.mult, ALU.add), t4)
        cn_tok = DV.op(C(dv.tensor_scalar, CTX[0:8, T:2 * T], CTX[0:8, 0:T], -1.0, None, ALU.mult), ct_tok)

        t1 = AC.op(C(ac.activation, GT, FG[:, :, 8:32].rearrange("p a (h b) -> p a h b", h=H), ACT.Tanh,
                                         scale=0.5), fg_tok)
        gate_tok = DV.op(C(dv.tensor_scalar, GT, GT, 0.5, 0.5, ALU.mult, ALU.add), t1)

        for i in range(4):
            b = pb()
            t = feat("nq", hA, 8, bank(b), free[b])
            free[b] = nq_tok = evac(NQ[:, i, :], bank(b), 0.125, t, eng=AC)

        kv_tok = []
        for i in range(2):
            b = pb()
            t = feat("kv", hA, 8, bank(b), free[b])
            X = XKV[i]
            t1 = DV.op(C(dv.tensor_copy, X[0:64, 0, :], bank(b)[0:64, :]), t)
            free[b] = t2 = DV.op(C(dv.tensor_copy, X[64:128, 1, 0:T - 1], bank(b)[64:128, 1:T]), t)
            free[b] = t3 = DV.op(C(dv.tensor_copy, OT[64:128, 0:1], bank(b)[64:128, 0:1]), t,
                                 kv_tok[-1] if kv_tok else None)
            kv_tok.append([PL.dma(X[64:128, 0, 0:T - 1], X[0:64, 0, 1:T], None, t1),
                           PL.dma(X[0:64, 1, 1:T], X[64:128, 1, 0:T - 1], None, t2),
                           PL.dma(X[0:64, 1, 0:1], OT[64:128, 0:1], None, t3), t2])
        ks_tok = {}
        for i, X in ((0, KS), (1, KW)):
            b = pb()
            t = feat("kv", hA, 8, bank(b), free[b])
            t1 = DV.op(C(dv.tensor_copy, X[0:64, 0, :], bank(b)[0:64, :]), t)
            free[b] = t2 = DV.op(C(dv.tensor_copy, X[64:128, 1, :], bank(b)[64:128, :]), t)
            a1 = PL.dma(X[64:128, 0, :], X[0:64, 0, :], None, t1)
            a2 = PL.dma(X[0:64, 1, :], X[64:128, 1, :], None, t2)
            ks_tok[i] = [t1, t2, a1, a2]
        kv_all = kv_tok

        pek, w2 = CS2[:, 0:32], CS2[:, 32:32 + 384]
        hT = [OB[0], OB[1]]
        ht_tok = {}
        kcT = SM[:, 200:262]
        vcm = SM[0:NC, 264:392].rearrange("p (g d) -> p g d", g=2)
        hc = SM[:, 400:404]
        hh = SM[:, 404:408]
        UU = OT
        for i, name in ((0, "w1k"), (1, "w1v")):
            PE.wait([free[b] for b in (2, 3, 4, 5)], ks_tok[1], kv_all, c2_tok)
            X = XKV[i]
            for tt in range(4):
                j, s = next_tile(name)
                w = s[:, :].rearrange("p (j c) -> p j c", j=4)
                for q in range(4):
                    jj = 4 * tt + q
                    rhs = X[:, :, 2 * jj:2 * jj + 481:16]
                    for c in range(2):
                        mm(bank(2 + c)[:, 0:62].rearrange("p (g n) -> p g n", g=2), w[:, q, 128 * c:128 * c + 128],
                           rhs, jj == 0, jj == 15)
                        last = mm(bank(4 + c)[:, 0:1], w[:, q, 128 * c:128 * c + 128],
                                  pek[:, 16 * i + jj:16 * i + jj + 1], jj == 0, jj == 15, inc=(c == 1 and q == 3))
                tile_done(j, last)
            for c in range(2):
                t1 = DV.op(C(dv.tensor_copy, hc[:, c:c + 1], bank(4 + c)[:, 0:1]), last, ht_tok.get("o"))
                t2 = DV.op(C(dv.tensor_scalar, hh[:, c:c + 1], bank(4 + c)[:, 0:1], 0.5, None, ALU.mult), last)
                free[4 + c] = t2
                t3 = AC.op(C(ac.activation, UU[:, 64 * c:64 * c + 62], bank(2 + c)[:, 0:62], ACT.Tanh,
                                                     scale=0.5, bias=hh[:, c:c + 1]), t2, kv_all)
                t4 = DV.op(C(dv.tensor_scalar, UU[:, 128 + 64 * c:190 + 64 * c], bank(2 + c)[:, 0:62],
                                                        hc[:, c:c + 1], None, ALU.add), t1, t3, kv_all)
                free[2 + c] = t4
                ht = DV.op(C(dv.scalar_tensor_tensor, 
                    out=hT[i][:, 64 * c:64 * c + 62], in0=UU[:, 64 * c:64 * c + 62], scalar=1.0,
                    in1=UU[:, 128 + 64 * c:190 + 64 * c], op0=ALU.add, op1=ALU.mult), t4, cn_tok)
            ht_tok["o"] = ht
            if i == 0:
                for c in range(2):
                    last = mm(bank(2)[:, 0:62], w2[:, 128 * c:128 * c + 128], hT[0][:, 64 * c:64 * c + 62],
                              c == 0, c == 1, ht, free[2], free[3], inc=True)
                free[2] = kc_tok = evac(kcT, bank(2)[:, 0:62], 0.5, last)
            else:
                for g in range(2):
                    for c in range(2):
                        last = mm(bank(2 + g)[0:NC, 0:64], hT[1][:, 64 * c + 31 * g:64 * c + 31 * g + 31],
                                  w2[:, 256 + 64 * c:320 + 64 * c], c == 0, c == 1, ht, free[2], free[3], inc=True)
                for g in range(2):
                    free[2 + g] = vc_tok = evac(vcm[:, g, :], bank(2 + g)[0:NC, 0:64], 0.5, last)

        ai = {"s": 0, "g": 0, "pt": 0, "e": 0}
        efree, pfree, ptfree = [None, None], [None, None], [None, None]
        obfree = [None, None]
        eb_tok = [arena_tok, arena_tok]
        for x in range(2):
            efree[x] = [arena_tok, cn_tok]
            pfree[x] = [arena_tok]
            ptfree[x] = [arena_tok]

        line, later = [], []

        def push(unit):
            line.append(unit)
            if unit:
                unit["a"]()
            if len(line) > 1 and line[-2]:
                line[-2]["b"]()
            if len(line) > 2 and line[-3]:
                line[-3]["c"]()
            for it in list(later):
                it[0] -= 1
                if it[0] <= 0:
                    later.remove(it)
                    it[1]()

        def flush():
            for _ in range(2):
                push(None)
            while later:
                later.pop(0)[1]()
            line.clear()

        def group(qT, kTf, bias, blocks, Vf, extra, toks, vtoks, done):
            g = ai["g"]
            ai["g"] += 1
            gs, ob = g % 4, 6 + g % 2
            n = blocks[-1][0] + blocks[-1][1]
            wide = n > T
            nslot = len(blocks)
            for h in range(H):
                u = {}

                def scores(h=h, u=u):
                    s = ai["s"] % 2
                    ai["s"] += 1
                    b = 2 if wide else 2 + s
                    S = PSF[:, b * 512:b * 512 + n]
                    PE.wait([free[2], free[3]] if wide else free[b], toks)
                    for c0, c1 in ([(0, T), (T, n)] if wide else [(0, n)]):
                        ex = extra(h, c0, c1) if extra else []
                        o = PSF[:, b * 512 + c0:b * 512 + c1]
                        last = mm(o, qT(h), kTf(h, c0, c1), True, not ex, inc=not ex)
                        for m, (l, r) in enumerate(ex):
                            last = mm(o, l, r, False, m == len(ex) - 1, inc=m == len(ex) - 1)
                    e = ai["e"] % 2
                    ai["e"] += 1
                    E, P = EB[e][:, 0:n], PB[e][:, 0:n]
                    t = DV.op(C(dv.tensor_tensor_reduce, E, S, bias(h), -1.0, 3e38, ALU.add, ALU.min,
                                nmx[gs][:, h:h + 1]), last, efree[e], gfree[gs])
                    free[b] = t
                    if wide:
                        free[3] = t
                    x = AC.op(C(ac.activation, P, E, ACT.Exp, bias=nmx[gs][:, h:h + 1], scale=-1.0,
                                accum_out=rsm[gs][:, h:h + 1]), t, pfree[e])
                    efree[e] = x
                    u.update(e=e, P=P, x=x)

                def turn(h=h, u=u):
                    big = nslot > 4
                    s = ai["pt"] % 2
                    ai["pt"] += 1
                    b = 4 if big else 4 + s
                    PE.wait([free[4], free[5]] if big else free[b], u["x"])
                    o0 = b * 512
                    for m, (c, w) in enumerate(blocks):
                        last = PE.op(C(pe.transpose, PSF[0:w, o0 + 128 * m:o0 + 128 * m + 128], u["P"][:, c:c + w],
                                       ident), inc=m == nslot - 1)
                    pfree[u["e"]] = last
                    pt = PTB[s]
                    tk = []
                    first = 0
                    q, cp = (AC, ac.copy) if s else (DV, dv.tensor_copy)
                    if blocks[0][1] < 128:
                        first = 1
                        w = blocks[0][1]
                        tk.append(q.op(C(cp, pt[0:w, 0:128], PSF[0:w, o0:o0 + 128]), last, ptfree[s]))
                    c0, c1 = 128 * first, 128 * nslot
                    tk.append(q.op(C(cp, pt[:, c0:c1], PSF[:, o0 + c0:o0 + c1]), last, ptfree[s]))
                    free[b] = list(tk)
                    if big:
                        free[5] = list(tk)
                    u.update(s=s, pt=pt, tk=tk)

                def values(h=h, u=u):
                    PE.wait(u["tk"], vtoks, free[ob] if h == 0 else None)
                    o = bank(ob)[:, 64 * h:64 * h + 64]
                    for m, (c, w) in enumerate(blocks):
                        pv = mm(o, u["pt"][0:w, 128 * m:128 * m + 128], Vf(h, m), m == 0, m == nslot - 1,
                                inc=m == nslot - 1)
                    ptfree[u["s"]] = pv
                    if h == H - 1:
                        done(pv, u["x"], ob, gs)

                u.update(a=scores, b=turn, c=values)
                push(u)

        gfree = [None] * 4

        def finish(pv, x, ob, gs, o, mult, toks, first=True, tmp=None):
            t = DV.op(C(dv.reciprocal, rcp[gs], rsm[gs]), x)
            if mult is not None:
                t = DV.op(C(dv.tensor_tensor, rcp[gs], rcp[gs], mult, ALU.mult), t, toks)
            dst = o if first else tmp
            t = DV.op(C(dv.tensor_tensor, 
                dst.rearrange("p (h d) -> p h d", h=H), bank(ob).rearrange("p (h d) -> p h d", h=H),
                rcp[gs][:, :].rearrange("p (h u) -> p h u", u=1).to_broadcast([128, H, HD]), ALU.mult), t, pv, toks)
            free[ob] = t
            gfree[gs] = t
            if not first:
                t = DV.op(C(dv.tensor_tensor, o, o, tmp, ALU.add), t)
            return t

        def to_B(o, qt, k0, tok, b):
            for m in range(4):
                last = PE.op(C(pe.transpose, bank(b)[:, 128 * m:128 * m + 128], o[:, 128 * m:128 * m + 128],
                                                      ident), tok, free[b], inc=m == 3)
            hi = Bh[:, k0:k0 + 4, 128 * qt:128 * qt + 128]
            lo = Bl[:, k0:k0 + 4, 128 * qt:128 * qt + 128]
            src = bank(b).rearrange("p (a c) -> p a c", a=4)
            a = AC.op(C(ac.copy, hi, src), last)
            c = DV.op(C(dv.tensor_tensor, lo, src, hi.bitcast(F), ALU.subtract), a)
            free[b] = [a, c]
            return last, [a, c]

        b_tok = []
        DV.wait(m_tok, bf_tok)
        NH_ = (lambda X: (lambda h: X[64 * (h % 2):64 * (h % 2) + 64, h // 2, :]))
        fqh, fkh, nqh = NH_(FQ), NH_(FK), NH_(NQ)
        obf = [[vc_tok, ht_tok["o"]], [vc_tok, ht_tok["o"]]]
        for qt in range(4):
            n = 128 * (qt + 1)
            q0 = 128 * qt

            def ext(h, c0, c1, q0=q0):
                return [(CTX[0:8, q0:q0 + 128], one_h[:, h:h + 1].to_broadcast([8, c1 - c0])),
                        (one_h[:, h:h + 1].to_broadcast([8, 128]), CTX[0:8, T + c0:T + c1])]

            def done(pv, x, ob, gs, qt=qt):
                O = OB[qt % 2]
                t = finish(pv, x, ob, gs, O, None, obf[qt % 2])

                def turn_out():
                    obf[qt % 2], bt = to_B(O, qt, 0, t, qt % 2)
                    b_tok.append(bt)

                later.append([3, turn_out])

            group(lambda h, q0=q0: fqh(h)[:, q0:q0 + 128], lambda h, a, b: fkh(h)[:, a:b],
                  lambda h, q0=q0: MK[:, 384 - q0:512], [(128 * m, 128) for m in range(qt + 1)],
                  lambda h, m: FV[:, m, 64 * h:64 * h + 64], ext,
                  [fq_tok, fk_tok, cn_tok], fv_toks, done)
        flush()

        OT2 = [FQ[:, 0, :], FQ[:, 1, :]]
        ON = [FQ[:, 2, :], FQ[:, 3, :], FK[:, 0, :], FK[:, 1, :]]
        alld_tok = [(PE.sem, PE.n), (DV.sem, DV.n)]
        onf = [None] * 4
        for qt in range(4):
            n = 128 * (qt + 1)
            q0 = 128 * qt
            O = ON[qt]
            g = ai["g"]
            ai["g"] += 1
            gs, ob = g % 4, 6 + g % 2
            PE.wait(free[2], free[3], kc_tok, nq_tok)
            for h in range(H):
                last = mm(bank(2 + h % 2)[:, 31 * (h // 2):31 * (h // 2) + 31], nqh(h)[:, q0:q0 + 128],
                          kcT[64 * (h % 2):64 * (h % 2) + 64, 31 * (h // 4):31 * (h // 4) + 31], True, True,
                          inc=h == H - 1)
            E = EB[0][:, 0:248].rearrange("p (h n) -> p h n", h=H)
            for w in range(2):
                t = DV.op(C(dv.tensor_tensor, E[:, w:H:2, :],
                            bank(2 + w)[:, 0:124].rearrange("p (h n) -> p h n", h=4), BC[:, qt, w:H:2, :], ALU.add),
                          last, efree[0], bc_tok)
                free[2 + w] = t
            t = DV.op(C(dv.tensor_reduce, nmx[gs], E, AX.X, ALU.max, negate=True), t, gfree[gs])
            t = DV.op(C(dv.tensor_tensor, 
                E, E, nmx[gs][:, :].rearrange("p (h u) -> p h u", u=1).to_broadcast([128, H, NC]), ALU.add), t)
            P = PB[0][:, 0:248]
            x = AC.op(C(ac.activation, P, EB[0][:, 0:248], ACT.Exp), t, pfree[0])
            efree[0] = x
            xs = DV.op(C(dv.tensor_reduce, rsm[gs], P.rearrange("p (h n) -> p h n", h=H), AX.X,
                                                           ALU.add), x)
            PE.wait(free[4], free[5], x)
            for h in range(H):
                last = PE.op(C(pe.transpose, PSF[0:NC, 2048 + 128 * h:2176 + 128 * h],
                                                           P[:, 31 * h:31 * h + 31], ident), inc=h == H - 1)
            pfree[0] = [last, xs]
            tk = []
            for s in range(2):
                tk.append(AC.op(C(ac.copy, PTB[s][0:NC, 0:512], bank(4 + s)[0:NC, :]), last, ptfree[s]))
                free[4 + s] = tk[-1]
            PE.wait(tk, vc_tok, free[ob])
            for h in range(H):
                pv = mm(bank(ob)[:, 64 * h:64 * h + 64], PTB[h // 4][0:NC, 128 * (h % 4):128 * (h % 4) + 128],
                        vcm[:, h // 4, :], True, True, inc=h == H - 1)
            ptfree = [pv, pv]
            vg = DV.op(C(dv.tensor_scalar, GT[:, qt, :, 0], GT[:, qt, :, 0], vals[:, qt:qt + 1], None,
                                                      ALU.mult), gate_tok)
            onf[qt] = finish(pv, xs, ob, gs, O, GT[:, qt, :, 0], [vg, alld_tok])
        for qt in range(4):
            q0 = 128 * qt
            for br, KX, v0 in ((1, KS, 0), (2, KW, 128)):
                def done(pv, x, ob, gs, qt=qt, br=br):
                    onf[qt] = t = finish(pv, x, ob, gs, ON[qt], GT[:, qt, :, br], [onf[qt], gate_tok], first=False,
                                         tmp=OT2[br - 1])

                    def turn_out():
                        _, bt = to_B(ON[qt], qt, 4, t, qt % 2)
                        b_tok.append(bt)

                    if br == 2:
                        later.append([3, turn_out])

                group(lambda h, q0=q0: nqh(h)[:, q0:q0 + 128],
                      lambda h, a, b, KX=KX: KX[64 * (h % 2):64 * (h % 2) + 64, h // 4, a:b],
                      lambda h, q0=q0: BFX[:, h, 384 - q0:512], [(128 * m, 128) for m in range(qt + 1)],
                      lambda h, m, v0=v0: V2[:, m, v0 + 64 * (h // 4):v0 + 64 * (h // 4) + 64], None,
                      [nq_tok, ks_tok[0], ks_tok[1]], [v2_tok], done)
        flush()

        def merge(names, brsrc, xtok, bt):
            M = AR[:, 0:4096].rearrange("p (k t) -> p k t", k=8)
            G = [AR[:, 4096 + 512 * i:4608 + 512 * i] for i in range(4)]
            T1 = [AR[:, 6144 + 512 * i:6656 + 512 * i] for i in range(4)]
            gf, tf = [None] * 4, [None] * 4
            mt = []
            ga, gb, br, wo, bg = names
            for i in range(8):
                tt = []
                for w, nm in ((0, ga), (1, gb)):
                    b = w + 4 * (i % 2)
                    sl = 2 * (i % 2) + w
                    t = feat(nm, hA, 8, bank(b), free[b])
                    if bg is None:
                        t1 = AC.op(C(ac.activation, G[sl], bank(b), ACT.Tanh, scale=0.5), t, gf[sl])
                    else:
                        t1 = AC.op(C(ac.activation, 
                            G[sl], bank(b), ACT.Tanh, scale=0.5, bias=bg[:, 8 * w + i:8 * w + i + 1]), t, gf[sl], bg_tok)
                    free[b] = t1
                    t2 = PL.op(C(pl.tensor_scalar, G[sl], G[sl], 0.5, 0.5, ALU.mult, ALU.add), t1)
                    tt.append(t2)
                j, p = next_tile(br)
                bb = [2 + 4 * (i % 2), 3 + 4 * (i % 2)]
                PE.wait(free[bb[0]], free[bb[1]], bt)
                for w in range(2):
                    for k in range(4):
                        kk = 4 * w + k
                        a, c = WH[p][:, kk * 128:kk * 128 + 128], WL[p][:, kk * 128:kk * 128 + 128]
                        s0, e = k == 0, k == 3
                        mm(bank(bb[w]), a, Bh[:, kk, :], s0, False)
                        mm(bank(bb[w]), a, Bl[:, kk, :], False, False)
                        last = mm(bank(bb[w]), c, Bh[:, kk, :], False, e, inc=e)
                tile_done(j, last)
                for w in range(2):
                    sl = 2 * (i % 2) + w
                    tf[sl] = DV.op(C(dv.tensor_tensor, T1[sl], G[sl], bank(bb[w]), ALU.mult),
                                   last, tt[w], tf[sl])
                    gf[sl] = free[bb[w]] = tf[sl]
                s0 = 2 * (i % 2)
                t = DV.op(C(dv.tensor_tensor, M[:, i, :], T1[s0], T1[s0 + 1], ALU.add),
                          tf[s0], tf[s0 + 1])
                tf[s0] = tf[s0 + 1] = t
                mt.append(t)
            pe_done = last
            km = {}
            for k in range(8):
                km[k] = split_to(Ah[:, k, 0:T], Al[:, k, 0:T], M[:, k, :], mt[k], pe_done)
            xt = []
            for i in range(8):
                b = pb()
                t = feat(wo, hA, 8, bank(b), free[b], kmap=km if i == 0 else None)
                free[b] = t1 = DV.op(C(dv.tensor_tensor, x3[:, i, 0:T], bank(b), x3[:, i, 0:T], ALU.add),
                                     t, xtok)
                xt.append(t1)
            return xt

        toks = barrier()
        x_tok = PL.dma(x3[:, :, 0:T], d["xT"], None, toks)
        xt = merge(("ga", "gb", "br", "wo", None), hB, x_tok, b_tok)
        toks = barrier()
        norm_to_A(T, gv[1], lambda k: [xt[k]], toks)

        RT = [AR[:, 4096 + 512 * i:4608 + 512 * i] for i in range(8)]
        rf = [None] * 8
        pe_b = None
        for q in range(4):
            km = {}
            for i in range(8):
                b = pb()
                t = feat("f1", hA, 8, bank(b), free[b], kmap=hk if q == 0 else None)
                sl = 2 * (i % 4)
                free[b] = t1 = AC.op(C(ac.activation, RT[sl], bank(b), ACT.Relu), t, rf[sl])
                t2 = DV.op(C(dv.tensor_tensor, RT[sl + 1], RT[sl], RT[sl], ALU.mult), t1, rf[sl + 1])
                rf[sl] = t2
                km[i] = split_to(Bh[:, i, :], Bl[:, i, :], RT[sl + 1], t2, pe_b)
                rf[sl + 1] = km[i]
            for i in range(8):
                b = pb()
                t = feat("f2", hB, 8, bank(b), free[b], kmap=km if i == 0 else None)
                free[b] = xt[i] = DV.op(C(dv.tensor_tensor, x3[:, i, 0:T], bank(b), x3[:, i, 0:T],
                                                                          ALU.add), t)
            pe_b = t

        toks = barrier()
        nx = rms(lambda k: x3[:, k, 0:T], 8, T, float(D), gv[5], lambda k, src, t: t, lambda k: [xt[k]],
                 AR[:, 0:7 * TM], 0, 1, dst=lambda k: x3[:, k, 0:T])
        xt = [nx[1]] * 8
        if d.get("x1") is not None:
            dbg = PL.dma(d["x1"], x3[:, :, 0:T], None, xt)
            DV.wait(dbg)

        toks = barrier()
        c2_tok = PL.dma(CS2[:, 0:296], d["cs2"], None, toks)
        bg_tok = DV.op(C(dv.tensor_scalar, CS2[:, 280:296], CS2[:, 280:296], 0.5, None, ALU.mult), c2_tok)
        meta_tok = PL.dma(x3[:, :, T:TM], d["meta"], None, toks)
        x2_tok = PL.dma(d["x2"], x3[:, :, 0:T], None, xt)
        hend = norm_to_A(TM, gv[2], lambda k: [xt[k], meta_tok], toks)
        kc0 = dict(hk)
        DV.wait(hend)
        AC.wait(hend)

        def v3(o, a, n):
            return AR[:, o:o + a * n].rearrange("p (a t) -> p a t", a=a)

        AQ = v3(0, 4, 512)
        QB = v3(2048, 4, 512)
        KB = v3(4096, 4, TM)
        VB = v3(6208, 4, 512)
        VBm = AR[0:NM, 8256:8768]
        BA = v3(8768, 8, 256)
        AK = v3(10816, 2, TM)
        AV = v3(11872, 4, 128)
        AVm = AR[0:NM, 12384:12512]
        IQ = v3(12512, 2, 512)
        IK = AR[:, 13536:14064]
        SCo = [14064, 14208, 14480, 14880]
        SCw = [144, 272, 400, 528]
        SMK = AR[:, 14064 + 1344:14064 + 1344 + 672].bitcast(BF)
        so = [0, 144, 416, 816]
        base = 14064 + 1344 + 672
        EB = [AR[:, base + 528 * i:base + 528 * i + 528] for i in range(2)]
        PB = [AR[:, base + 1056 + 528 * i:base + 1056 + 528 * i + 528] for i in range(2)]
        PTB = [AR[:, base + 2112 + 640 * i:base + 2112 + 640 * i + 640] for i in range(2)]
        OB = [AR[:, base + 3392:base + 3904], CTX[:, 0:512]]
        OT = CTX[:, 512:1024]
        SM = AR[:, base + 3904:20288]
        nmx = [SM[:, 8 * i:8 * i + 8] for i in range(4)]
        rsm = [SM[:, 32 + 8 * i:40 + 8 * i] for i in range(4)]
        rcp = [SM[:, 64 + 8 * i:72 + 8 * i] for i in range(4)]
        IW = SM[:, 96:112].rearrange("p (a t) -> p a t", a=4)
        mx8 = [SM[:, 112 + 8 * i:120 + 8 * i] for i in range(4)]
        BBX = XT[:, :].rearrange("p (h t) -> p h t", h=H)

        ba_tok = toep(BA, 8, 399, 256, toks, hend)
        bb_tok = toep(BBX, 16, 127, TM, hend, x2_tok)
        t = tokmajor("ik", None, 196, (5, 3), mt=True, mbank=4)
        IN_ = OB[0]
        ikn = [EB[0][:, 128 * i:128 * i + 128] for i in range(4)] + [EB[1][:, 0:128]]
        st6 = SM[:, 144:144 + 30].rearrange("p (a s) -> p a s", a=5)
        mv = SM[:, 176:186].rearrange("p (a s) -> p a s", a=5)
        rs = SM[:, 186:196].rearrange("p (a s) -> p a s", a=5)
        PE.wait(t)
        for a in range(5):
            b, np_ = a, (128 if a < 4 else NM)
            B = bank(b)
            if a < 4:
                t1 = DV.op(C(dv.tensor_copy, AV[:, a, :], B[:, 0:128]), t)
                t1 = DV.op(C(dv.tensor_scalar, IW[:, a, :], B[:, 192:196], 0.0625, None, ALU.mult), t)
            else:
                t1 = DV.op(C(dv.tensor_copy, AVm, B[0:NM, 0:128]), t)
            av_tok = iw_tok = t1
            x_ = ikn[a][0:np_, 64:128]
            t1 = DV.op(C(dv.tensor_copy, x_, B[0:np_, 128:192]), t)
            free[b] = t1
            m = mv[0:np_, a, :]
            r_ = rs[0:np_, a, :]
            c_ = ikn[a][0:np_, 0:64]
            t2 = DV.op(C(dv.tensor_reduce, m[:, 0:1], x_, AX.X, ALU.add), t1)
            t2 = DV.op(C(dv.tensor_scalar, m[:, 0:1], m[:, 0:1], -1.0 / 64, None, ALU.mult), t2)
            t2 = DV.op(C(dv.tensor_scalar, x_, x_, m[:, 0:1], None, ALU.add), t2)
            t2 = AC.op(C(ac.activation, c_, x_, ACT.Square, accum_out=m[:, 1:2]), t2)
            t2 = DV.op(C(dv.tensor_scalar, m[:, 1:2], m[:, 1:2], 1.0 / 64, EPS, ALU.mult, ALU.add), t2)
            t3 = AC.op(C(ac.activation, r_[:, 0:1], m[:, 1:2], ACT.Ln), t2)
            t3 = AC.op(C(ac.activation, r_[:, 0:1], r_[:, 0:1], ACT.Exp, scale=-0.5), t3)
            t3 = DV.op(C(dv.tensor_tensor, r_[:, 1:2], r_[:, 0:1], r_[:, 0:1], ALU.mult), t3)
            t3 = DV.op(C(dv.scalar_tensor_tensor, out=r_[:, 1:2], in0=r_[:, 1:2], scalar=-0.5,
                                                                  in1=m[:, 1:2], op0=ALU.mult, op1=ALU.mult), t3)
            t3 = DV.op(C(dv.scalar_tensor_tensor, out=r_[:, 0:1], in0=r_[:, 1:2], scalar=1.5,
                                                                  in1=r_[:, 0:1], op0=ALU.add, op1=ALU.mult), t3)
            t4 = DV.op(C(dv.scalar_tensor_tensor, 
                out=x_, in0=x_, scalar=r_[:, 0:1], in1=CS2[0:np_, 0:64], op0=ALU.mult, op1=ALU.mult), t3, c2_tok)
            t4 = DV.op(C(dv.tensor_tensor, x_, x_, CS2[0:np_, 64:128], ALU.add), t4)
            t4 = DV.op(C(dv.tensor_copy, c_, x_), t4)
            last = PE.op(C(pe.transpose, 
                bank(5)[:, 128 * (a % 4):128 * (a % 4) + np_] if a < 4 else bank(6)[:, 0:NM],
                ikn[a][0:np_, :], ident[0:np_, 0:np_]), t4, free[5], free[6])
        ik_tok = DV.op(C(dv.tensor_copy, IK[:, NM:TM], bank(5)), last)
        free[5] = ik_tok
        ik_tok = DV.op(C(dv.tensor_copy, IK[:, 0:NM], bank(6)[:, 0:NM]), last)
        free[6] = ik_tok
        for i in range(2):
            b = pb()
            t = feat("iq", hA, 8, bank(b), free[b])
            free[b] = iq_tok = evac(IQ[:, i, :], bank(b), 1.0, t, eng=AC)
        sc_tok = [None] * 4
        rl = [PB[0], PB[1]]
        rlf = [None, None]
        n_ = [0]
        for qt in (3, 2, 1, 0):
            w = SCw[qt]
            S = AR[:, SCo[qt]:SCo[qt] + w]
            tk = None
            for h in range(4):
                s = n_[0] % 2
                n_[0] += 1
                b = 2 + 2 * s
                PE.wait(free[b], free[b + 1], iq_tok, ik_tok)
                hb = 64 * (h % 2)
                for c0, c1 in ([(0, w)] if w <= T else [(0, T), (T, w)]):
                    last = mm(PSF[:, b * 512 + c0:b * 512 + c1], IQ[hb:hb + 64, h // 2, 128 * qt:128 * qt + 128],
                              IK[hb:hb + 64, c0:c1], True, True, inc=True)
                t1 = AC.op(C(ac.activation, rl[s][:, 0:w], PSF[:, b * 512:b * 512 + w], ACT.Relu),
                           last, rlf[s])
                free[b] = free[b + 1] = t1
                if h == 0:
                    tk = DV.op(C(dv.scalar_tensor_tensor, out=S[:, w - 144:w], in0=rl[s][:, w - 144:w],
                                 scalar=IW[:, qt, 0:1], in1=CS2[:, 128:272], op0=ALU.mult, op1=ALU.add),
                               t1, iw_tok, c2_tok)
                    if w > 144:
                        tk = DV.op(C(dv.tensor_scalar, S[:, 0:w - 144], rl[s][:, 0:w - 144], IW[:, qt, 0:1], None,
                                     ALU.mult), t1)
                else:
                    tk = DV.op(C(dv.scalar_tensor_tensor, 
                        out=S, in0=rl[s][:, 0:w], scalar=IW[:, qt, h:h + 1], in1=S,
                        op0=ALU.mult, op1=ALU.add), t1, tk)
                rlf[s] = tk
            sc_tok[qt] = tk

        b = pb()
        t = feat("bkv", hA, 8, bank(b), free[b], free[4], om=bank(4)[:, 0:NM])
        ckr = PTB[0][:, 0:TM]
        t1 = DV.op(C(dv.tensor_copy, ckr[:, 0:T], bank(b)), t)
        free[b] = t1
        t1 = DV.op(C(dv.tensor_copy, ckr[:, T:TM], bank(4)[:, 0:NM]), t)
        free[4] = t1
        bqr = VB[:, 0:2, :]
        for i in range(2):
            b = pb()
            t = feat("bq", hA, 8, bank(b), free[b])
            free[b] = bq_tok = DV.op(C(dv.tensor_copy, bqr[:, i, :], bank(b)), t)
        tmpn = AR[:, 0:7 * TM]

        ck2 = {}

        def put_ck(k, src, tt):
            ck2[0] = split_to(Bh[:, 2:4, :].rearrange("p a t -> p (a t)")[:, 0:TM],
                              Bl[:, 2:4, :].rearrange("p a t -> p (a t)")[:, 0:TM], src, tt)
            return ck2[0]

        r1 = rms(lambda k: ckr, 1, TM, 128.0, kvn, put_ck, lambda k: [t1], tmpn, 0, 1)
        PE.wait(r1)
        AC.wait(ck2[0])
        DV.wait(ck2[0])
        bq2 = {}

        def put_bq(k, src, tt):
            bq2[k] = split_to(Bh[:, k, :], Bl[:, k, :], src, tt)
            return bq2[k]

        rms(lambda k: bqr[:, k, :], 2, T, 256.0, qn, put_bq, lambda k: [bq_tok], tmpn, 0, 1)
        AC.wait(bq2[1])
        DV.wait(bq2[1])

        b = pb()
        t = feat("ak", hA, 8, bank(b), free[b], free[4], om=bank(4)[:, 0:NM])
        t1 = DV.op(C(dv.tensor_copy, AK[0:64, 0, NM:TM], bank(b)[0:64, :]), t)
        t2 = DV.op(C(dv.tensor_copy, AK[64:128, 1, NM:TM], bank(b)[64:128, :]), t)
        free[b] = t2
        t1 = DV.op(C(dv.tensor_copy, AK[0:64, 0, 0:NM], bank(4)[0:64, 0:NM]), t)
        t2 = DV.op(C(dv.tensor_copy, AK[64:128, 1, 0:NM], bank(4)[64:128, 0:NM]), t)
        free[4] = t2
        ak_tok = [t2, PL.dma(AK[64:128, 0, :], AK[0:64, 0, :], None, t1), PL.dma(AK[0:64, 1, :], AK[64:128, 1, :], None, t2)]
        for i in range(4):
            b = pb()
            t = feat("aq", hA, 8, bank(b), free[b])
            free[b] = aq_tok = evac(AQ[:, i, :], bank(b), 0.125, t, bq2[1], eng=AC)
        j, p = next_tile("uq")
        for i in range(4):
            b = pb()
            PE.wait(free[b], bq2[0], bq2[1])
            for k in range(2):
                a, c = WH[p][:, 512 * k + 128 * i:512 * k + 128 * i + 128], WL[p][:, 512 * k + 128 * i:512 * k + 128 * i + 128]
                mm(bank(b), a, Bh[:, k, :], k == 0, False)
                mm(bank(b), a, Bl[:, k, :], False, False)
                last = mm(bank(b), c, Bh[:, k, :], False, k == 1, inc=k == 1)
            free[b] = qb_tok = evac(QB[:, i, :], bank(b), 0.125, last, eng=AC)
        tile_done(j, last)
        j, p = next_tile("ukv")
        ckh = Bh[:, 2:4, :].rearrange("p a t -> p (a t)")
        ckl = Bl[:, 2:4, :].rearrange("p a t -> p (a t)")
        PE.wait(ck2[0])
        for i in range(4):
            b = pb()
            a, c = WH[p][:, 128 * i:128 * i + 128], WL[p][:, 128 * i:128 * i + 128]
            for o, x0, x1, bb in ((bank(b), 0, T, b), (bank(4)[:, 0:NM], T, TM, 4)):
                PE.wait(free[bb])
                mm(o, a, ckh[:, x0:x1], True, False)
                mm(o, a, ckl[:, x0:x1], False, False)
                last = mm(o, c, ckh[:, x0:x1], False, True, inc=True)
            free[b] = evac(KB[:, i, NM:TM], bank(b), 1.0, last)
            free[4] = kb_tok = evac(KB[:, i, 0:NM], bank(4)[:, 0:NM], 1.0, last)
        for a in range(5):
            b = pb()
            np_ = 128 if a < 4 else NM
            c0 = 128 * a if a < 4 else T
            wa, wb = WH[p][:, 512:1024], WL[p][:, 512:1024]
            PE.wait(free[b])
            mm(bank(b)[0:np_, :], ckh[:, c0:c0 + np_], wa, True, False)
            mm(bank(b)[0:np_, :], ckl[:, c0:c0 + np_], wa, False, False)
            last = mm(bank(b)[0:np_, :], ckh[:, c0:c0 + np_], wb, False, True, inc=True)
            free[b] = vb_tok = evac(VB[:, a, :] if a < 4 else VBm, bank(b)[0:np_, :], 1.0, last)
        tile_done(j, last)
        ckb_tok = last

        al_tok = [(e.sem, e.n) for e in (PE, DV, AC)]
        efree = [al_tok, al_tok]
        pfree = [al_tok, al_tok]
        ptfree = [al_tok, al_tok]
        gfree = [None] * 4
        obf = [al_tok, al_tok]
        aqh, qbh = NH_(AQ), NH_(QB)
        kbh = NH_(KB)
        b_tok = []
        DV.wait(ba_tok, bb_tok)

        rounds = {qt: sc_tok[qt] for qt in range(4)}

        def topk_round(last):
            for qt in (3, 2, 1, 0):
                S = AR[:, SCo[qt]:SCo[qt] + SCw[qt]]
                t1 = DV.op(C(dv.max, mx8[qt], S), rounds[qt])
                rounds[qt] = t1
            for qt in (3, 2, 1, 0):
                S = AR[:, SCo[qt]:SCo[qt] + SCw[qt]]
                rounds[qt] = DV.op(C(dv.match_replace, S, mx8[qt], S, NREP), rounds[qt])

        for i in range(16):
            topk_round(i == 15)
        for qt in range(4):
            S = AR[:, SCo[qt]:SCo[qt] + SCw[qt]]
            sm_tok = DV.op(C(dv.tensor_scalar, SMK[:, so[qt]:so[qt] + SCw[qt]], S, -2e38, NEG,
                                                               ALU.is_gt, ALU.mult), rounds[qt])

        for qt in range(4):
            q0 = 128 * qt
            kst = 0 if qt == 0 else q0 - 112
            if qt == 0:
                blocks = [(0, NM), (NM, 128)]
            else:
                blocks = [(0, 128), (128, 128)]

            def vA(h, m, qt=qt):
                c = 64 * (h // 4)
                if qt == 0 and m == 0:
                    return AVm[:, c:c + 64]
                return AV[:, qt - 1 + m, c:c + 64]

            def done(pv, x, ob, gs, qt=qt):
                O = OB[qt % 2]
                sk = CS2[:, 272:280]
                wk = SM[:, 200 + 24 * (qt % 2):224 + 24 * (qt % 2)]
                t = DV.op(C(dv.tensor_tensor, wk[:, 0:8], sk, nmx[gs], ALU.add), x, c2_tok)
                t = DV.op(C(dv.tensor_scalar, wk[:, 8:16], wk[:, 0:8], 0.0, None, ALU.max), t)
                t = DV.op(C(dv.tensor_tensor, wk[:, 0:8], wk[:, 0:8], wk[:, 8:16], ALU.subtract), t)
                ta = AC.op(C(ac.activation, wk[:, 0:8], wk[:, 0:8], ACT.Exp), t)
                tb = AC.op(C(ac.activation, wk[:, 8:16], wk[:, 8:16], ACT.Exp, scale=-1.0), t)
                t = DV.op(C(dv.tensor_tensor, rsm[gs], rsm[gs], wk[:, 8:16], ALU.mult), tb, x)
                t = DV.op(C(dv.tensor_tensor, rsm[gs], rsm[gs], wk[:, 0:8], ALU.add), t, ta)
                t = finish(pv, t, ob, gs, O, wk[:, 8:16], obf[qt % 2])

                def turn_out():
                    obf[qt % 2], bt = to_B(O, qt, 0, [t, ckb_tok], qt % 2)
                    b_tok.append(bt)

                later.append([3, turn_out])

            group(lambda h, q0=q0: aqh(h)[:, q0:q0 + 128],
                  lambda h, a, b, kst=kst: AK[64 * (h % 2):64 * (h % 2) + 64, h // 4, kst + a:kst + b],
                  lambda h, qt=qt: BA[:, h, 112 if qt == 0 else 0:256], blocks, vA, None,
                  [aq_tok, ak_tok, ba_tok], [av_tok], done)
        flush()

        for qt in range(4):
            q0 = 128 * qt
            n = NM + 128 * (qt + 1)
            blocks = [(0, NM)] + [(NM + 128 * m, 128) for m in range(qt + 1)]

            def ext2(h, c0, c1, qt=qt):
                return [(IDB[:, :], SMK[:, so[qt] + c0:so[qt] + c1])]

            def done(pv, x, ob, gs, qt=qt):
                O = OB[qt % 2]
                t = finish(pv, x, ob, gs, O, None, obf[qt % 2])

                def turn_out():
                    obf[qt % 2], bt = to_B(O, qt, 4, t, qt % 2)
                    b_tok.append(bt)

                later.append([3, turn_out])

            group(lambda h, q0=q0: qbh(h)[:, q0:q0 + 128], lambda h, a, b: kbh(h)[:, a:b],
                  lambda h, q0=q0: BBX[:, h, 384 - q0:TM], blocks,
                  lambda h, m: VBm[:, 64 * h:64 * h + 64] if m == 0 else VB[:, m - 1, 64 * h:64 * h + 64],
                  ext2, [qb_tok, kb_tok, sm_tok, bb_tok, idb_tok], [vb_tok], done)
        flush()

        toks = barrier()
        x_tok = PL.dma(x3[:, :, 0:T], d["x2"], None, toks, x2_tok)
        xt = merge(("ga2", "gb2", "br2", "wo2", CS2[:, 280:296]), hB, x_tok, b_tok)
        toks = barrier()
        norm_to_A(T, gv[3], lambda k: [xt[k]], toks)
        rf = [None] * 8
        pe_b = None
        for ci, n in enumerate(SIZES2):
            km = {}
            for i in range(n):
                b = 2 * (i % 2)
                tg = feat("fg", hA, 8, bank(b), free[b], kmap=hk if ci == 0 else None)
                tu = feat("fu", hA, 8, bank(b + 1), free[b + 1])
                sl = 2 * (i % 4)
                t1 = AC.op(C(ac.activation, RT[sl], bank(b), ACT.Tanh, scale=0.5), tg, rf[sl])
                t2 = DV.op(C(dv.scalar_tensor_tensor, 
                    out=RT[sl], in0=RT[sl], scalar=1.0, in1=bank(b), op0=ALU.add, op1=ALU.mult), t1, tg)
                free[b] = t2
                t3 = DV.op(C(dv.scalar_tensor_tensor, 
                    out=RT[sl + 1], in0=RT[sl], scalar=0.5, in1=bank(b + 1), op0=ALU.mult, op1=ALU.mult),
                    t2, tu, rf[sl + 1])
                free[b + 1] = rf[sl] = t3
                km[i] = split_to(Bh[:, i, :], Bl[:, i, :], RT[sl + 1], t3, pe_b)
                rf[sl + 1] = km[i]
            for i in range(8):
                b = pb()
                t = feat("fd", hB, n, bank(b), free[b], kmap=km if i == 0 else None)
                free[b] = xt[i] = DV.op(C(dv.tensor_tensor, x3[:, i, 0:T], bank(b), x3[:, i, 0:T],
                                                                          ALU.add), t)
            pe_b = t
        toks = barrier()
        def put_out(k, src, t):
            return PL.dma(out[k, :, :], src, outs[k % 2], t)

        outs = [dsem("s_out0"), dsem("s_out1")]
        rms(lambda k: x3[:, k, 0:T], 8, T, float(D), gv[4], put_out, lambda k: [xt[k]], AR[:, 0:7 * TM], 0, 1)
        PL.wait((outs[0][0], outs[0][1]), (outs[1][0], outs[1][1]))
        assert st["use"] == len(tiles)

        with nc.Block() as block:
            for q, reg in ((SP, block.sync), (PE, block.tensor), (DV, block.vector), (AC, block.scalar),
                           (PL, block.gpsimd)):
                def run(e, q=q):
                    for fn in q.q:
                        fn()
                reg(run)


def columns(w, c0, n=128):
    k = w.shape[0] // 128
    return w[:, c0:c0 + n].reshape(k, 128, n).transpose(1, 0, 2).reshape(128, k * n)


def rows(w, k0, nk):
    n = w.shape[1]
    return w[128 * k0:128 * (k0 + nk)].reshape(nk, 128, n).transpose(1, 0, 2).reshape(128, nk * n)


def bucket(n):
    large = 16 + (np.log(np.maximum(n, 16) / 16.0) / np.log(8.0) * 16).astype(np.int64)
    return np.where(n < 16, n, np.minimum(large, 31))


def one_hot(dist):
    o = np.zeros((34, dist.size), np.float32)
    ok = dist >= 0
    o[bucket(np.maximum(dist, 0))[ok], np.nonzero(ok)[0]] = 1.0
    o[32, ~ok] = NEG
    o[33, dist >= 128] = NEG
    return o


def layout(a):
    w_in, w2 = a["w_in"][0], a["w_in_2"][0]
    tiles = tile_list()
    pack = np.zeros((len(tiles), 128, 1024), np.float32)
    a2 = np.concatenate([w_in[:, 2440:2568], w_in[:, 2696:2824], w_in[:, 1536:1544], w_in[:, 2824:2848]], axis=1)
    ik = np.concatenate([w2[:, 640:768], w2[:, 1408:1472], w2[:, 1472:1476]], axis=1)
    col = {"fq": (w_in, 0), "fk": (w_in, 512), "nq": (w_in, 1544), "ga": (w_in, 2848), "gb": (w_in, 3872),
           "wo": (a["w_out"][0], 0), "f1": (a["w_ff1"][0], 0), "aq": (w2, 0), "bq": (w2, 768), "bkv": (w2, 1024),
           "iq": (w2, 1152), "ak": (w2, 512), "ga2": (w2, 1476), "gb2": (w2, 2500), "wo2": (a["w_out_2"][0], 0),
           "fg": (a["w_ffn_gate_2"][0], 0), "fu": (a["w_ffn_up_2"][0], 0)}
    kv = (2056, 2184, 2312, 2568)
    for j, (name, i, n, _) in enumerate(tiles):
        if name in col:
            w, c0 = col[name]
            t = columns(w, c0 + 128 * i)
        elif name == "kv":
            t = columns(w_in, kv[i])
        elif name == "fv":
            t = rows(w_in[:, 1024:1536], 2 * i, 2)
        elif name == "a2":
            t = rows(a2, 3 * i, n // 288)
        elif name == "ik":
            t = rows(ik, 5 * i, n // 196)
        elif name in ("w1k", "w1v"):
            t = rows(a["cmp_w1_k" if name == "w1k" else "cmp_w1_v"][0], 4 * i, 4)
        elif name == "br":
            t = np.concatenate([columns(a["w_br_fox"][0], 128 * i), columns(a["w_br_nsa"][0], 128 * i)], axis=1)
        elif name == "br2":
            t = np.concatenate([columns(a["w_branch_a_2"][0], 128 * i), columns(a["w_branch_b_2"][0], 128 * i)],
                               axis=1)
        elif name == "f2":
            q, f = divmod(i, 8)
            t = columns(a["w_ff2"][0][1024 * q:1024 * q + 1024], 128 * f)
        elif name == "fd":
            c, f = divmod(i, 8)
            t = columns(a["w_ffn_down_2"][0][1024 * c:1024 * c + n], 128 * f)
        elif name == "uq":
            t = rows(a["w_uq_2"][0], 0, 2)
        else:
            t = np.concatenate([a["w_uk_2"][0].reshape(128, 512), a["w_uv_2"][0].reshape(128, 512)], axis=1)
        pack[j, :, 0:n] = t

    def chunks(v):
        return v.reshape(-1, 128).transpose(1, 0)

    def fm(x):
        return np.ascontiguousarray(x.reshape(x.shape[0], 8, 128).transpose(2, 1, 0))

    cst = np.zeros((128, 196), np.float32)
    cst[:, 0:128] = np.eye(128)
    for i, g in enumerate((a["g_attn"][0], a["g_mlp"][0], a["attn_norm_g_2"][0], a["ffn_norm_g_2"][0],
                           a["final_norm_g_2"], a["g_final"])):
        cst[:, 128 + 8 * i:136 + 8 * i] = chunks(g)
    cst[0:8, 178:186] = np.eye(8)
    cst[0:8, 186] = a["b_forget"][0]
    cst[:, 187:191] = 1.0
    cst[0:31, 187] = 0.0
    cst[:, 192:194] = chunks(a["q_norm_g_2"][0])
    cst[:, 194:195] = chunks(a["kv_norm_g_2"][0])
    cs1 = np.zeros((128, 416), np.float32)
    cs1[:, 0:16] = chunks(a["cmp_pe_k"][0].reshape(-1))
    cs1[:, 16:32] = chunks(a["cmp_pe_v"][0].reshape(-1))
    for c in range(2):
        w = a["cmp_w2_k"][0][128 * c:128 * c + 128]
        cs1[:, 32 + 128 * c:96 + 128 * c] = w
        cs1[:, 96 + 128 * c:160 + 128 * c] = w
        cs1[:, 288 + 64 * c:352 + 64 * c] = a["cmp_w2_v"][0][128 * c:128 * c + 128]
    cs2 = np.zeros((128, 296), np.float32)
    cs2[:, 0:64] = a["idx_k_ln_g_2"][0]
    cs2[:, 64:128] = a["idx_k_ln_b_2"][0]
    q, j = np.arange(128)[:, None], np.arange(144)[None, :]
    cs2[:, 128:272] = np.where(j > 16 + q, np.float32(NADM), np.float32(0.0))
    cs2[:, 272:280] = a["sinks_2"][0]
    cs2[:, 280:296] = chunks(a["b_gates_2"][0])
    mk = np.where(np.arange(T)[None, :] - 384 > q, np.float32(NEG), np.float32(0.0))
    tab = np.zeros((34, 24), np.float32)
    tab[0:32, 0:8] = a["rel_bias_table"]
    tab[0:32, 8:24] = a["rel_bias_2"]
    tab[32] = 1.0
    tab[33, 8:16] = 1.0
    return {"w": pack, "xT": fm(a["x"][0]), "meta": fm(a["meta_tokens_2"]), "cst": cst, "cs1": cs1, "cs2": cs2,
            "mk": mk, "tab": tab, "ohf": one_hot(np.arange(NOH) - 511), "ohr": one_hot(527 - np.arange(NR_))}


def kernel(**inputs):
    import concourse.bacc as bacc
    from concourse.bass_utils import run_bass_kernel_spmd

    arrays = layout({k: np.asarray(v) for k, v in inputs.items()})
    nc = bacc.Bacc("TRN2", target_bir_lowering=False, num_devices=1)
    d = {k: nc.dram_tensor(k + "_in", v.shape, F, kind="ExternalInput").ap() for k, v in arrays.items()}
    d["scr"] = nc.dram_tensor("scr_tmp", (24, 16, NR_), F, kind="Internal").ap()
    d["x2"] = nc.dram_tensor("x2_tmp", (128, 8, T), F, kind="Internal").ap()
    out = nc.dram_tensor("out_0", (8, 128, T), F, kind="ExternalOutput").ap()
    build(nc, d, out)
    r = run_bass_kernel_spmd(nc, [{k + "_in": v for k, v in arrays.items()}], core_ids=[0])
    y = r.results[0]["out_0"]
    return np.ascontiguousarray(y.reshape(D, T).transpose(1, 0)).reshape(1, T, D)
```

```python
from contextlib import ExitStack

import numpy as np

import concourse.bass as bass
from concourse import mybir

F = mybir.dt.float32
R = mybir.dt.float32r
BF = mybir.dt.bfloat16
ALU = mybir.AluOpType
ACT = mybir.ActivationFunctionType
AX = mybir.AxisListType

T = 512
NM = 16
TM = T + NM
D = 1024
H = 8
HD = 64
NC = 31
RAW = 4
SPL = 3
NEG = -1e30
NADM = -1e37
NREP = -3e38
EPS = 1e-6
NOH = 992
NR_ = 672
SIZES2 = (8, 8, 6)


def tile_list():
    t = []
    t += [("fq", i, 1024, True) for i in range(4)]
    t += [("fk", i, 1024, True) for i in range(4)]
    t += [("fv", i, 1024, True) for i in range(4)]
    t += [("a2", i, 288 * n, True) for i, n in enumerate((3, 3, 2))]
    t += [("nq", i, 1024, True) for i in range(4)]
    t += [("kv", i, 1024, True) for i in range(4)]
    t += [("w1k", i, 1024, False) for i in range(4)]
    t += [("w1v", i, 1024, False) for i in range(4)]
    for i in range(8):
        t += [("ga", i, 1024, True), ("gb", i, 1024, True), ("br", i, 1024, True)]
    t += [("wo", i, 1024, True) for i in range(8)]
    for q in range(4):
        t += [("f1", 8 * q + i, 1024, True) for i in range(8)]
        t += [("f2", 8 * q + i, 1024, True) for i in range(8)]
    t += [("ik", i, 196 * n, True) for i, n in enumerate((5, 3))]
    t += [("iq", i, 1024, True) for i in range(2)]
    t += [("bkv", 0, 1024, True)]
    t += [("bq", i, 1024, True) for i in range(2)]
    t += [("ak", 0, 1024, True)]
    t += [("aq", i, 1024, True) for i in range(4)]
    t += [("uq", 0, 1024, True), ("ukv", 0, 1024, True)]
    for i in range(8):
        t += [("ga2", i, 1024, True), ("gb2", i, 1024, True), ("br2", i, 1024, True)]
    t += [("wo2", i, 1024, True) for i in range(8)]
    f = 0
    for c, n in enumerate(SIZES2):
        for i in range(n):
            t += [("fg", f + i, 1024, True), ("fu", f + i, 1024, True)]
        t += [("fd", 8 * c + i, n * 128, True) for i in range(8)]
        f += n
    return t


def C(fn, *args, **kw):
    return lambda: fn(*args, **kw)


def build(nc, d, out):
    tiles = tile_list()
    with ExitStack() as ctx:
        def sb(name, shape, dt=F):
            return ctx.enter_context(nc.sbuf_tensor(name, shape, dt))

        def sem(name):
            return ctx.enter_context(nc.semaphore(name))

        nds = [0]

        class Queue:

            def __init__(self, name, eng):
                self.eng, self.sem, self.n, self.q, self.seen = eng, sem(name), 0, [], {}

            def wait(self, *toks):
                for tok in toks:
                    if tok is None:
                        continue
                    if isinstance(tok, list):
                        self.wait(*tok)
                        continue
                    s, v = tok
                    if self.seen.get(id(s), 0) < v:
                        self.seen[id(s)] = v
                        self.q.append(lambda s=s, v=v: self.eng.wait_ge(s, v))

            def op(self, fn, *toks, inc=True):
                self.wait(*toks)
                if not inc:
                    self.q.append(fn)
                    return None
                self.n += 1
                self.q.append(lambda: fn().then_inc(self.sem, 1))
                return (self.sem, self.n)

            def dma(self, dst, src, ds, *toks):
                self.wait(*toks)
                if ds is None:
                    nds[0] += 1
                    ds = [sem(f"s_dma{nds[0]}"), 0]
                self.q.append(lambda: self.eng.dma_start(dst, src).then_inc(ds[0], 16))
                ds[1] += 16
                return (ds[0], ds[1])

        PE = Queue("s_pe", nc.tensor)
        DV = Queue("s_dv", nc.vector)
        AC = Queue("s_ac", nc.scalar)
        PL = Queue("s_pl", nc.gpsimd)
        SP = Queue("s_sp", nc.sync)
        pe, dv, ac, pl = nc.tensor, nc.vector, nc.scalar, nc.gpsimd

        def dsem(name):
            return [sem(name), 0]

        Ah, Al = sb("Ah", [128, 8, TM], R), sb("Al", [128, 8, TM], R)
        Bh, Bl = sb("Bh", [128, 8, T], R), sb("Bl", [128, 8, T], R)
        WH = [sb(f"WH{i}", [128, 1024], R) for i in range(SPL)]
        WL = [sb(f"WL{i}", [128, 1024], R) for i in range(SPL)]
        WR = [sb(f"WR{i}", [128, 1024]) for i in range(RAW)]
        XT = sb("XT", [128, 8 * TM])
        AR = sb("AR", [128, 20288])
        CTX = sb("CTX", [128, 2 * T])
        CS2 = sb("CS2", [128, 416])
        CST = sb("CST", [128, 196])
        ONE = sb("ONE", [128, 1])
        NS = sb("NS", [128, 25])
        IDB = sb("IDB", [128, 128], BF)
        PSA = ctx.enter_context(nc.psum_tensor("PSA", [128, 8, 512], F))
        PSF = PSA[:, :, :].rearrange("p b c -> p (b c)")

        def bank(i):
            return PSA[:, i, :]

        ident = CST[:, 0:128]
        gv = [CST[:, 128 + 8 * i:136 + 8 * i] for i in range(6)]
        one_h = CST[0:104, 178:186]
        bfor = CST[0:104, 186:187]
        vals = CST[:, 187:191]
        qn = CST[:, 192:194]
        kvn = CST[:, 194:195]

        c_tok = SP.dma(CST[:, :], d["cst"], None)
        c2_tok = PL.dma(CS2[:, 0:416], d["cs1"], None)
        one_tok = DV.op(C(dv.memset, ONE[:, :], 1.0))
        idb_tok = DV.op(C(dv.memset, NS[:, :], 1.0))
        idb_tok = DV.op(C(dv.tensor_copy, IDB[:, :], ident), c_tok)
        x3 = XT[:, :].rearrange("p (k t) -> p k t", k=8)
        x_tok = [SP.dma(x3[:, 2 * k:2 * k + 2, 0:T], d["xT"][:, 2 * k:2 * k + 2, :], None) for k in range(4)]

        raw_sem = [dsem(f"s_raw{i}") for i in range(RAW)]
        raw_free = [None] * RAW
        split_free = [None] * SPL
        loaded, ready = {}, {}
        st = {"dma": 0, "split": 0, "use": 0, "ns": 0}

        def load_tile():
            j = st["dma"]
            if j >= len(tiles):
                return
            st["dma"] += 1
            s, n = j % RAW, tiles[j][2]
            loaded[j] = SP.dma(WR[s][:, 0:n], d["w"][j, :, 0:n], raw_sem[s], raw_free[s])

        for _ in range(RAW):
            load_tile()

        def split_tile():
            j = st["split"]
            if j >= len(tiles):
                return
            st["split"] += 1
            name, _, n, split = tiles[j]
            s = j % RAW
            if not split:
                ready[j] = ([loaded[j]], WR[s], None)
                return
            p = st["ns"] % SPL
            st["ns"] += 1
            hi = AC.op(C(ac.copy, WH[p][:, 0:n], WR[s][:, 0:n]), loaded[j], split_free[p])
            q, e = (PL, pl) if name in ("bkv", "bq", "ak", "aq", "uq", "ukv") else (DV, dv)
            lo = q.op(C(e.tensor_tensor, WL[p][:, 0:n], WR[s][:, 0:n], WH[p][:, 0:n].bitcast(F), ALU.subtract),
                       hi, loaded[j], split_free[p])
            raw_free[s] = [hi, lo]
            ready[j] = ([hi, lo], p, None)
            load_tile()

        idle_dv = []

        def run_idle(n):
            for _ in range(min(n, len(idle_dv))):
                idle_dv.pop(0)()

        def next_tile(name, ahead=True):
            j = st["use"]
            assert tiles[j][0] == name, (tiles[j], name)
            st["use"] += 1
            while st["split"] <= j + (SPL - 1 if tiles[j][3] and ahead else 0) and st["split"] < len(tiles):
                if st["split"] > j and not (tiles[st["split"]][3] and tiles[j][3]):
                    break
                split_tile()
            run_idle(10)
            PE.wait(ready[j][0])
            return j, ready[j][1]

        def tile_done(j, tok):
            if tiles[j][3]:
                split_free[ready[j][1]] = tok
            else:
                raw_free[j % RAW] = tok
                load_tile()

        def mm(o, l, r, start, stop, *toks, inc=False):
            return PE.op(C(pe.matmul, o, l, r, start=start, stop=stop), *toks, inc=inc)

        def feat(name, src, nk, o, *toks, kmap=None, ncol=T, cols=None, om=None, skip0=0):
            j, p = next_tile(name)
            PE.wait(*toks)
            w = cols or (lambda W, k: W[:, k * 128:(k + 1) * 128])
            sh, sl = src
            for k in range(nk):
                PE.wait(kmap[k] if kmap else None)
                a, b = w(WH[p], k), w(WL[p], k)
                s0, e = k == 0, k == nk - 1
                mm(o, a, sh(k, 0, T), s0, False)
                mm(o, a, sl(k, 0, T), False, False)
                last = mm(o, b, sh(k, 0, T), False, e, inc=e)
            if om is not None:
                for k in range(nk):
                    a, b = w(WH[p], k), w(WL[p], k)
                    s0, e = k == 0, k == nk - 1
                    mm(om, a, sh(k, T, TM), s0, False)
                    mm(om, a, sl(k, T, TM), False, False)
                    last = mm(om, b, sh(k, T, TM), False, e, inc=e)
            tile_done(j, last)
            return last

        def feat2(names, src, o, waits, kmap):
            ts = [next_tile(names[0]), next_tile(names[1], ahead=False)]
            PE.wait(*waits)
            sh, sl = src
            last = [None, None]
            for k in range(8):
                PE.wait(kmap[k])
                for i, (j, p) in enumerate(ts):
                    a, b = WH[p][:, k * 128:(k + 1) * 128], WL[p][:, k * 128:(k + 1) * 128]
                    mm(o[i], a, sh(k, 0, T), k == 0, False)
                    mm(o[i], a, sl(k, 0, T), False, False)
                    last[i] = mm(o[i], b, sh(k, 0, T), False, k == 7, inc=k == 7)
            for (j, p), t in zip(ts, last):
                tile_done(j, t)
            return last

        def feats(name, n, src, kmap):
            start = 0
            if kmap:
                b = [pb(), pb()]
                tk = feat2((name, name), src, [bank(b[0]), bank(b[1])], [free[b[0]], free[b[1]]], kmap)
                for i in range(2):
                    yield i, b[i], tk[i]
                start = 2
            for i in range(start, n):
                b = pb()
                yield i, b, feat(name, src, 8, bank(b), free[b])

        nb = [0]

        def pb():
            nb[0] += 1
            return nb[0] % 2

        hA = (lambda k, a, b: Ah[:, k, a:b], lambda k, a, b: Al[:, k, a:b])
        hB = (lambda k, a, b: Bh[:, k, a:b], lambda k, a, b: Bl[:, k, a:b])

        def queued():
            return [(e.sem, e.n) for e in (PE, DV, AC, PL) if e.n]

        free = [None] * 8

        class Norm:

            def __init__(self, X, nk, width, n, gcol, put, tmp, b0, b1, dst=None, held=None):
                self.X, self.nk, self.width, self.n, self.gcol, self.put = X, nk, width, n, gcol, put
                self.tmp, self.b0, self.b1, self.dst = tmp, b0, b1, dst
                self.acc = [tmp[:, 0:TM], tmp[:, TM:2 * TM]]
                self.sq = [tmp[:, 2 * TM:3 * TM], tmp[:, 3 * TM:4 * TM]]
                self.hb = [tmp[:, 4 * TM:5 * TM], tmp[:, 5 * TM:6 * TM]]
                self.held = held if held is not None else {}
                self.sqf, self.at, self.xt = [None, None], [None, None], {}

            def stat(self, k, *toks):
                W, s = slice(0, self.width), k % 2
                if k == 7:
                    AC.op(C(ac.activation, NS[:, 24:25], ONE[:, 0:1], ACT.Ln), one_tok)
                self.xt[k] = list(toks)
                dst = self.acc[k] if k < 2 else self.sq[s][:, W]
                dst = dst[:, W] if k < 2 else dst
                a = AC.op(C(ac.activation, dst, self.X(k), ACT.Square), *toks,
                          self.sqf[s] if k >= 2 else self.held.get("acc"))
                if k >= 2:
                    q, e = (PL, pl) if s == 0 else (DV, dv)
                    a = q.op(C(e.tensor_tensor, self.acc[s][:, W], self.acc[s][:, W], self.sq[s][:, W], ALU.add), a,
                             self.at[s])
                    self.sqf[s] = a
                self.at[s] = a

            def finish(self):
                self.sums()
                return self.scale()

            def sums(self):
                width, b0 = self.width, self.b0
                na = (width + 127) // 128
                b1 = self.b1
                PE.wait(free[b0], free[b1], one_tok, idb_tok)
                m = min(self.nk, 2)
                for i in range(m):
                    PE.wait(self.at[i])
                    for a in range(na):
                        c0, c1 = 128 * a, min(128 * a + 128, width)
                        last = mm(bank((b0, b1)[i])[0:c1 - c0, a:a + 1], self.acc[i][:, c0:c1], ONE[:, 0:1], True, True,
                                  inc=True)
                self.held["acc"] = last
                v, r, u = NS[:, 0:na], NS[:, 8:8 + na], NS[:, 16:16 + na]
                pieces = [(slice(0, 128), slice(0, width // 128))]
                if width % 128:
                    pieces.append((slice(0, width % 128), slice(na - 1, na)))
                t = self.held.get("ns")
                for ps, cs in pieces:
                    t = DV.op(C(dv.tensor_scalar, v[ps, cs], bank(b0)[ps, cs], 1.0 / self.n, EPS, ALU.mult, ALU.add),
                              last, t)
                    if m == 2:
                        t = DV.op(C(dv.scalar_tensor_tensor, out=v[ps, cs], in0=bank(b1)[ps, cs], scalar=1.0 / self.n,
                                    in1=v[ps, cs], op0=ALU.mult, op1=ALU.add), t)
                free[b0] = free[b1] = t
                t1 = AC.op(C(ac.activation, r, v, ACT.Ln), t)
                t1 = AC.op(C(ac.activation, r, r, ACT.Exp, scale=-0.5), t1)
                t2 = DV.op(C(dv.tensor_tensor, u, r, r, ALU.mult), t1)
                t2 = DV.op(C(dv.scalar_tensor_tensor, out=u, in0=u, scalar=-0.5, in1=v, op0=ALU.mult, op1=ALU.mult), t2)
                t2 = DV.op(C(dv.scalar_tensor_tensor, out=r, in0=u, scalar=1.5, in1=r, op0=ALU.add, op1=ALU.mult), t2)
                self.t2, self.r, self.na = t2, r, na

            def scale(self):
                width, b0, b1, t2, r, na = self.width, self.b0, self.b1, self.t2, self.r, self.na
                PE.wait(t2, free[b0], free[b1] if width > T else None, c_tok)
                for a in range(na):
                    n = min(128, width - 128 * a)
                    o = bank(b0)[:, 128 * a:128 * a + n] if a < 4 else bank(b1)[:, 0:n]
                    last = mm(o, r[0:n, a:a + 1].to_broadcast([n, 128]), ident[0:n, 0:n], True, True, inc=True)
                self.held["ns"] = last
                if width > T:
                    assert b1 == b0 + 1
                RB = PSF[:, b0 * 512:b0 * 512 + width]
                W = slice(0, width)
                hf = self.held.setdefault("hf", [None, None])
                for k in range(self.nk):
                    t = DV.op(C(dv.scalar_tensor_tensor, out=self.dst(k) if self.dst else self.hb[k % 2][:, W],
                                in0=self.X(k), scalar=self.gcol[:, k:k + 1], in1=RB, op0=ALU.mult, op1=ALU.mult),
                              last, hf[k % 2] if not self.dst else None, self.xt[k])
                    if k:
                        hf[(k - 1) % 2] = self.put(k - 1, self.hb[(k - 1) % 2][:, W], tp)
                    tp = t
                k = self.nk - 1
                hf[k % 2] = self.put(k, self.hb[k % 2][:, W], tp)
                if self.dst:
                    self.held["hf"] = [None, None]
                free[b0] = t
                if width > T:
                    free[b1] = t
                return [x for x in hf if x]

        def split_to(hi, lo, src, tok, *toks, pool=False):
            a = AC.op(C(ac.copy, hi, src), tok, *toks)
            if pool:
                return [a, PL.op(C(pl.tensor_tensor, lo, src, hi.bitcast(F), ALU.subtract), a)]
            b = DV.op(C(dv.tensor_tensor, lo, src, hi.bitcast(F), ALU.subtract), a)
            return [a, b]

        hk = {}

        def put_A(width):
            def put(k, src, t):
                hk[k] = split_to(Ah[:, k, 0:width], Al[:, k, 0:width], src, t, pool=k % 2 == 1)
                return hk[k]

            return put

        NT = AR[:, 8192:8192 + 6 * TM]
        held = {}

        def norm_to_A(width, gcol):
            return Norm(lambda k: x3[:, k, 0:width], 8, width, float(D), gcol, put_A(width), NT, 6, 7, held=held)

        def evac(o, i, scale, tok, *toks, eng=None):
            if eng is AC:
                return AC.op(C(ac.activation, o, i, ACT.Copy, scale=scale), tok, *toks)
            return DV.op(C(dv.tensor_scalar, o, i, scale, None, ALU.mult), tok, *toks)

        OHF = AR[0:34, 14944:14944 + NOH]
        OHR = AR[0:34, 15968:15968 + NR_]
        TB = AR[0:34, 16992:17016]
        MK = AR[:, 14432:14944]
        o_tok = [PL.dma(OHF, d["ohf"], None), PL.dma(OHR, d["ohr"], None), PL.dma(TB, d["tab"], None)]
        m_tok = PL.dma(MK, d["mk"], None)
        nrm = norm_to_A(T, gv[0])
        for k in range(8):
            nrm.stat(k, x_tok[k // 2])

        FQ, FK = AR[:, 0:2048].rearrange("p (a t) -> p a t", a=4), AR[:, 2048:4096].rearrange("p (a t) -> p a t", a=4)
        FV = AR[:, 4096:6144].rearrange("p (a t) -> p a t", a=4)
        XKV = [AR[:, 6144 + 1024 * i:7168 + 1024 * i].rearrange("p (g t) -> p g t", g=2) for i in range(2)]
        NQ = AR[:, 8192:10240].rearrange("p (a t) -> p a t", a=4)
        KS = AR[:, 10240:11264].rearrange("p (g t) -> p g t", g=2)
        KW = AR[:, 11264:12288].rearrange("p (g t) -> p g t", g=2)
        V2 = AR[:, 12288:13312].rearrange("p (a t) -> p a t", a=4)
        FG = AR[:, 13312:13440].rearrange("p (a t) -> p a t", a=4)
        BC = AR[:, 13440:14432].rearrange("p (a h n) -> p a h n", a=4, h=H)
        BCF = AR[:, 13440:14432].rearrange("p (u n) -> p u n", u=4 * H)
        MK = AR[:, 14432:14944]
        EB = [AR[:, 14944 + 528 * i:15472 + 528 * i] for i in range(4)]
        PTB = [AR[:, 17056 + 640 * i:17696 + 640 * i] for i in range(2)]
        OB = [AR[:, 18336 + 512 * i:18848 + 512 * i] for i in range(2)]
        OT = AR[:, 19360:19872]
        SM = AR[:, 19872:20288]
        nmx = [SM[:, 8 * i:8 * i + 8] for i in range(4)]
        rsm = [SM[:, 32 + 8 * i:40 + 8 * i] for i in range(4)]
        rcp = [SM[:, 64 + 8 * i:72 + 8 * i] for i in range(4)]
        GT = SM[:, 96:192].rearrange("p (a h b) -> p a h b", a=4, h=H)
        BFX = XT[:, 0:4096].rearrange("p (h t) -> p h t", h=H)

        OHF = AR[0:34, 14944:14944 + NOH]
        OHR = AR[0:34, 15968:15968 + NR_]
        TB = AR[0:34, 16992:17016]
        GR = AR[0:24, 17056:17056 + NR_]
        GC = AR[0:8, 17728:18720]
        for c in range(2):
            last = mm(bank(4 + c)[0:24, 0:336], TB, OHR[:, 336 * c:336 * c + 336], True, True, o_tok, inc=True)
        gt = None
        for c in range(2):
            gt = DV.op(C(dv.tensor_copy, GR[:, 336 * c:336 * c + 336], bank(4 + c)[0:24, 0:336]), last)
            free[4 + c] = gt
        for c in range(2):
            last = mm(bank(2 + c)[0:8, 0:496], TB[:, 0:8], OHF[:, 496 * c:496 * c + 496], True, True, inc=True)
        for c in range(2):
            lt = DV.op(C(dv.tensor_copy, GC[:, 496 * c:496 * c + 496], bank(2 + c)[0:8, 0:496]), last)
            free[2 + c] = lt
        for _ in range(2):
            split_tile()
        done = nrm.finish()
        g_tok = PL.dma(d["scr"], GR[:, :].rearrange("p (u m) -> p u m", u=1).to_broadcast([24, 16, NR_]), None, gt)
        gc_tok = [PL.dma(bass.AP(tensor=d["scr2"].tensor, offset=7992 * a, ap=[[1000, 8], [1, 992]]), GC, None, lt)
                  for a in range(4)]
        bc_tok = []
        for a in range(8):
            src = bass.AP(tensor=d["scr2"].tensor, offset=7 - a, ap=[[62, 16], [1000, 4 * H], [1, NC]])
            bc_tok.append(PL.dma(BCF[16 * a:16 * a + 16, :, :], src, None, gc_tok))

        def toep(dst, c0, base, width, *toks):
            tk = []
            for a in range(8):
                src = bass.AP(tensor=d["scr"].tensor, offset=c0 * 16 * NR_ + base - 16 * a,
                              ap=[[NR_ - 1, 16], [16 * NR_, H], [1, width]])
                tk.append(PL.dma(dst[16 * a:16 * a + 16, :, :], src, None, *toks))
            return tk

        bf_tok = toep(BFX, 0, 143, T, g_tok, done)
        arena_tok = [done, last, gt, g_tok, gc_tok]

        AC.wait(done)
        DV.wait(done)
        for i, b, t in feats("fq", 4, hA, dict(hk)):
            free[b] = fq_tok = evac(FQ[:, i, :], bank(b), 0.125, t, eng=AC)
        for i in range(4):
            b = pb()
            t = feat("fk", hA, 8, bank(b), free[b])
            free[b] = fk_tok = evac(FK[:, i, :], bank(b), 1.0, t)

        def tokmajor(name, widths, n, ks, mt=False, banks=(0, 1, 2, 3), mbank=None):
            k = 0
            for q, cnt in enumerate(ks):
                j, p = next_tile(name)
                PE.wait(*[free[b] for b in banks], free[mbank] if mt else None)
                for kk in range(cnt):
                    kx = k + kk
                    PE.wait(hk[kx])
                    s0, e = kx == 0, kx == 7
                    wa, wb = WH[p][:, kk * n:(kk + 1) * n], WL[p][:, kk * n:(kk + 1) * n]
                    for a in range(5 if mt else 4):
                        c0, c1 = 128 * a, min(128 * a + 128, TM)
                        o = bank(banks[a] if a < 4 else mbank)[0:c1 - c0, 0:n]
                        h1, l1 = Ah[:, kx, c0:c1], Al[:, kx, c0:c1]
                        mm(o, h1, wa, s0, False)
                        mm(o, l1, wa, False, False)
                        last = mm(o, h1, wb, False, e, inc=kk == cnt - 1)
                tile_done(j, last)
                k += cnt
            return last

        t = tokmajor("fv", None, 512, (2, 2, 2, 2))
        for a in range(4):
            free[a] = fv_tok = evac(FV[:, a, :], bank(a), 1.0, t, eng=AC if a % 2 else DV)
        fv_toks = [free[2], free[3]]
        t = tokmajor("a2", None, 288, (3, 3, 2))
        for a in range(4):
            t1 = evac(V2[:, a, :], bank(a)[:, 0:256], 1.0, t)
            free[a] = fg_tok = DV.op(C(dv.tensor_copy, FG[:, a, :], bank(a)[:, 256:288]), t)
        v2_tok = fg_tok
        LF = OB[0][0:104, :]
        LT = OB[1][0:104, :]
        FX = AR[:, 17056:17472].rearrange("p (a t) -> p a t", a=4)
        t1 = DV.op(C(dv.memset, FX, 0.0), arena_tok)
        for c0 in (0, 32, 64, 96):
            t1 = DV.op(C(dv.tensor_copy, FX[:, :, c0:c0 + 8], FG[:, :, 0:8]), fg_tok, t1)
        for a in range(4):
            last = PE.op(C(pe.transpose, bank(4)[0:104, 128 * a:128 * a + 128], FX[:, a, :], ident),
                         t1, free[4], c_tok)
        t1 = DV.op(C(dv.tensor_scalar, LF, bank(4)[0:104, :], bfor, None, ALU.add), last, arena_tok)
        free[4] = t1
        t2 = DV.op(C(dv.scalar_tensor_tensor, out=LT, in0=LF, scalar=-1.0, in1=LF, op0=ALU.mult, op1=ALU.max), t1)
        t3 = AC.op(C(ac.activation, LT, LT, ACT.Exp, scale=-1.0), t2)
        t3 = AC.op(C(ac.activation, LT, LT, ACT.Ln, bias=1.0), t3)
        t4 = DV.op(C(dv.scalar_tensor_tensor, out=LF, in0=LF, scalar=0.0, in1=LT, op0=ALU.min,
                                                   op1=ALU.subtract), t3)
        t4 = DV.op(C(dv.memset, LT, 1.0), t4)
        ct_tok = DV.op(C(dv.tensor_tensor_scan, CTX[0:104, 0:T], LT, LF, 0.0, ALU.mult, ALU.add), t4)
        t1 = DV.op(C(dv.tensor_scalar, CTX[0:104, T:2 * T], CTX[0:104, 0:T], -1.0, None, ALU.mult), ct_tok)
        CR = Bh[0:104, 4:6, :].rearrange("p a t -> p (a t)")
        C1 = Bh[0:104, 6, 0:8]
        t2 = AC.op(C(ac.copy, CR, CTX[0:104, :]), t1)
        AC.op(C(ac.copy, C1, one_h), c_tok)
        for r in (32, 96):
            cn_tok = DV.op(C(dv.tensor_tensor, CR[r:r + 8, :], CTX[r:r + 8, :], CR[r:r + 8, :].bitcast(F), ALU.subtract),
                           t2, (AC.sem, AC.n))

        t1 = AC.op(C(ac.activation, GT, FG[:, :, 8:32].rearrange("p a (h b) -> p a h b", h=H), ACT.Tanh,
                                         scale=0.5), fg_tok)
        gate_tok = DV.op(C(dv.tensor_scalar, GT, GT, 0.5, 0.5, ALU.mult, ALU.add), t1)

        for i in range(4):
            b = pb()
            t = feat("nq", hA, 8, bank(b), free[b])
            free[b] = nq_tok = evac(NQ[:, i, :], bank(b), 0.125, t, eng=AC)

        kv_tok = []
        for i in range(2):
            b = pb()
            t = feat("kv", hA, 8, bank(b), free[b])
            X = XKV[i]
            t1 = DV.op(C(dv.tensor_copy, X[0:64, 0, :], bank(b)[0:64, :]), t)
            free[b] = t2 = DV.op(C(dv.tensor_copy, X[64:128, 1, 0:T - 1], bank(b)[64:128, 1:T]), t)
            free[b] = t3 = DV.op(C(dv.tensor_copy, OT[64:128, 0:1], bank(b)[64:128, 0:1]), t,
                                 kv_tok[-1] if kv_tok else None)
            kv_tok.append([PL.dma(X[64:128, 0, 0:T - 1], X[0:64, 0, 1:T], None, t1),
                           PL.dma(X[0:64, 1, 1:T], X[64:128, 1, 0:T - 1], None, t2),
                           PL.dma(X[0:64, 1, 0:1], OT[64:128, 0:1], None, t3), t2])
        ks_tok = {}
        XP = [AR[:, 14944 + 992 * i:15936 + 992 * i] for i in range(2)]
        pek = CS2[:, 0:32]
        xp_tok = []
        for i, X in ((0, KS), (1, KW)):
            b = pb()
            t = feat("kv", hA, 8, bank(b), free[b])
            t1 = DV.op(C(dv.tensor_copy, X[0:64, 0, :], bank(b)[0:64, :]), t)
            free[b] = t2 = DV.op(C(dv.tensor_copy, X[64:128, 1, :], bank(b)[64:128, :]), t)
            a1 = PL.dma(X[64:128, 0, :], X[0:64, 0, :], None, t1)
            a2 = PL.dma(X[0:64, 1, :], X[64:128, 1, :], None, t2)
            ks_tok[i] = [t1, t2, a1, a2]
            for jj in range(16):
                t = DV.op(C(dv.tensor_scalar, XP[i][:, 62 * jj:62 * jj + 62].rearrange("p (g n) -> p g n", g=2),
                            XKV[i][:, :, 2 * jj:2 * jj + 481:16], pek[:, 16 * i + jj:16 * i + jj + 1], None, ALU.add),
                          kv_tok[i], c2_tok, arena_tok)
            xp_tok.append(t)
        kv_all = kv_tok

        def halves(tensors):
            return lambda i: tensors[i // 2][:, 512 * (i % 2):512 * (i % 2) + 512]

        def cut_in(hi, lo, src, n, *toks):
            tk = []
            for i in range(n):
                tk.append(split_to(hi(i), lo(i), src(i), None, *toks))
            return tk

        def hsel(f, h):
            return slice(64 * (h % 2), 64 * (h % 2) + 64)

        qh, ql = halves((WH[0], WH[1])), halves((WL[0], WL[1]))
        kh = halves((WH[2], WL[2]))
        k2l = lambda i: Bl[:, 4 + i, :]
        f_tok = cut_in(kh, k2l, lambda i: FK[:, i, :], 4, *split_free, fk_tok, fq_tok)
        f_tok += cut_in(qh, ql, lambda i: FQ[:, i, :], 4)
        NH_ = (lambda X: (lambda h: X[64 * (h % 2):64 * (h % 2) + 64, h // 2, :]))
        fqh, fkh, nqh = NH_(FQ), NH_(FK), NH_(NQ)
        obf = [cn_tok, cn_tok]
        w2 = CS2[:, 32:32 + 384]
        HP = [AR[0:62, 6144 + 256 * i:6400 + 256 * i] for i in range(2)]
        hT = [AR[:, 6656 + 128 * i:6784 + 128 * i] for i in range(2)]
        kcT = SM[:, 200:262]
        vcm = SM[0:NC, 264:392].rearrange("p (g d) -> p g d", g=2)
        UU = OT[0:62, 0:256]
        ht = None
        for i, name in ((0, "w1k"), (1, "w1v")):
            PE.wait(free[2 + i], xp_tok[i])
            for tt in range(4):
                j, s = next_tile(name)
                for q in range(4):
                    jj = 4 * tt + q
                    last = mm(bank(2 + i)[0:62, 0:256], XP[i][:, 62 * jj:62 * jj + 62], s[:, 256 * q:256 * q + 256],
                              jj == 0, jj == 15, inc=q == 3)
                tile_done(j, last)
            t1 = AC.op(C(ac.activation, UU, bank(2 + i)[0:62, 0:256], ACT.Tanh, scale=0.5), last, ht, kv_all)
            ht = DV.op(C(dv.scalar_tensor_tensor, out=HP[i], in0=UU, scalar=1.0, in1=bank(2 + i)[0:62, 0:256],
                         op0=ALU.add, op1=ALU.mult), t1, xp_tok[1])
            free[2 + i] = ht
        w1_tok = last
        kc_tok = vc_tok = None

        def compress_end():
            nonlocal kc_tok, vc_tok
            for i in range(2):
                PE.wait(ht, free[4 + i])
                for c in range(2):
                    last = PE.op(C(pe.transpose, bank(4 + i)[:, 64 * c:64 * c + 62], HP[i][:, 128 * c:128 * c + 128],
                                   ident[0:62, 0:62]))
                free[4 + i] = ht_t = DV.op(C(
                    dv.tensor_copy, hT[i].rearrange("p (c n) -> p c n", c=2)[:, :, 0:62],
                    bank(4 + i)[:, 0:128].rearrange("p (c n) -> p c n", c=2)[:, :, 0:62]), last)
            for c in range(2):
                last = mm(bank(2)[:, 0:62], w2[:, 128 * c:128 * c + 128], hT[0][:, 64 * c:64 * c + 62],
                          c == 0, c == 1, ht_t, free[2], inc=True)
            free[2] = kc_tok = evac(kcT, bank(2)[:, 0:62], 0.5, last)
            for g in range(2):
                for c in range(2):
                    last = mm(bank(3)[0:NC, 64 * g:64 * g + 64], hT[1][:, 64 * c + 31 * g:64 * c + 31 * g + 31],
                              w2[:, 256 + 64 * c:320 + 64 * c], c == 0, c == 1, free[3], inc=True)
            free[3] = vc_tok = evac(vcm, bank(3)[0:NC, 0:128].rearrange("p (g d) -> p g d", g=2), 0.5, last)

        ai = {"s": 0, "g": 0, "pt": 0, "e": 0}
        obfree = [None, None]
        eb_tok = [arena_tok, arena_tok]
        efree = [[arena_tok, cn_tok, w1_tok] for _ in range(4)]
        ptfree = [[arena_tok, w1_tok], [arena_tok, w1_tok]]

        line, later = [], []

        def push(unit):
            run_idle(2)
            line.append(unit)
            if unit:
                unit["a"]()
            if len(line) > 2 and line[-3]:
                line[-3]["b"]()
            if len(line) > 3 and line[-4]:
                line[-4]["c"]()
            for it in list(later):
                it[0] -= 1
                if it[0] <= 0:
                    later.remove(it)
                    it[1]()

        def flush():
            for _ in range(3):
                push(None)
            while later:
                later.pop(0)[1]()
            line.clear()

        def group(qT, kTf, bias, blocks, Vf, extra, toks, vtoks, done):
            g = ai["g"]
            ai["g"] += 1
            gs, ob = g % 4, 6 + g % 2
            n = blocks[-1][0] + blocks[-1][1]
            wide = n > T
            nslot = len(blocks)
            for h in range(H):
                u = {}

                def scores(h=h, u=u):
                    s = ai["s"] % 2
                    ai["s"] += 1
                    b = 2 * s if wide else 2 + s
                    S = PSF[:, b * 512:b * 512 + n]
                    PE.wait([free[b], free[b + 1]] if wide else free[b], toks)
                    for c0, c1 in ([(0, T), (T, n)] if wide else [(0, n)]):
                        ex = extra(h, c0, c1) if extra else []
                        o = PSF[:, b * 512 + c0:b * 512 + c1]
                        q, k = qT(h), kTf(h, c0, c1)
                        if isinstance(q, tuple):
                            ex = [(q[0], k[0]), (q[1], k[0]), (q[0], k[1])] + ex
                        else:
                            ex = [(q, k)] + ex
                        for m, (l, r) in enumerate(ex):
                            last = mm(o, l, r, m == 0, m == len(ex) - 1, inc=m == len(ex) - 1)
                    e = ai["e"] % 4
                    ai["e"] += 1
                    E = P = EB[e][:, 0:n]
                    t = DV.op(C(dv.tensor_tensor_reduce, E, S, bias(h), -1.0, 3e38, ALU.add, ALU.min,
                                nmx[gs][:, h:h + 1]), last, efree[e], gfree[gs])
                    free[b] = t
                    if wide:
                        free[b + 1] = t
                    x = AC.op(C(ac.activation, P, E, ACT.Exp, bias=nmx[gs][:, h:h + 1], scale=-1.0,
                                accum_out=rsm[gs][:, h:h + 1]), t)
                    u.update(e=e, P=P, x=x)

                def turn(h=h, u=u):
                    big = nslot > 4
                    s = ai["pt"] % 2
                    ai["pt"] += 1
                    b = 4 if big else 4 + s
                    PE.wait([free[4], free[5]] if big else free[b], u["x"])
                    o0 = b * 512
                    for m, (c, w) in enumerate(blocks):
                        last = PE.op(C(pe.transpose, PSF[0:w, o0 + 128 * m:o0 + 128 * m + 128], u["P"][:, c:c + w],
                                       ident), inc=m == nslot - 1)
                    efree[u["e"]] = last
                    pt = PTB[s]
                    tk = []
                    first = 0
                    q, cp = (AC, ac.copy) if s else (DV, dv.tensor_copy)
                    if blocks[0][1] < 128:
                        first = 1
                        w = blocks[0][1]
                        tk.append(q.op(C(cp, pt[0:w, 0:128], PSF[0:w, o0:o0 + 128]), last, ptfree[s]))
                    c0, c1 = 128 * first, 128 * nslot
                    tk.append(q.op(C(cp, pt[:, c0:c1], PSF[:, o0 + c0:o0 + c1]), last, ptfree[s]))
                    free[b] = list(tk)
                    if big:
                        free[5] = list(tk)
                    u.update(s=s, pt=pt, tk=tk)

                def values(h=h, u=u):
                    PE.wait(u["tk"], vtoks, free[ob] if h == 0 else None)
                    o = bank(ob)[:, 64 * h:64 * h + 64]
                    for m, (c, w) in enumerate(blocks):
                        pv = mm(o, u["pt"][0:w, 128 * m:128 * m + 128], Vf(h, m), m == 0, m == nslot - 1,
                                inc=m == nslot - 1)
                    ptfree[u["s"]] = pv
                    if h == H - 1:
                        done(pv, u["x"], ob, gs)

                u.update(a=scores, b=turn, c=values)
                push(u)

        gfree = [None] * 4

        def finish(pv, x, ob, gs, o, mult, toks, first=True, tmp=None):
            t = DV.op(C(dv.reciprocal, rcp[gs], rsm[gs]), x)
            if mult is not None:
                t = DV.op(C(dv.tensor_tensor, rcp[gs], rcp[gs], mult, ALU.mult), t, toks)
            dst = o if first else tmp
            t = DV.op(C(dv.tensor_tensor, 
                dst.rearrange("p (h d) -> p h d", h=H), bank(ob).rearrange("p (h d) -> p h d", h=H),
                rcp[gs][:, :].rearrange("p (h u) -> p h u", u=1).to_broadcast([128, H, HD]), ALU.mult), t, pv, toks)
            free[ob] = t
            gfree[gs] = t
            if not first:
                t = DV.op(C(dv.tensor_tensor, o, o, tmp, ALU.add), t)
            return t

        def to_B(o, qt, k0, tok, b):
            for m in range(4):
                last = PE.op(C(pe.transpose, bank(b)[:, 128 * m:128 * m + 128], o[:, 128 * m:128 * m + 128],
                                                      ident), tok, free[b], inc=m == 3)
            hi = Bh[:, k0:k0 + 4, 128 * qt:128 * qt + 128]
            lo = Bl[:, k0:k0 + 4, 128 * qt:128 * qt + 128]
            src = bank(b).rearrange("p (a c) -> p a c", a=4)
            a = AC.op(C(ac.copy, hi, src), last)
            c = DV.op(C(dv.tensor_tensor, lo, src, hi.bitcast(F), ALU.subtract), a)
            free[b] = [a, c]
            return last, [a, c]

        b_tok = []
        DV.wait(m_tok, bf_tok)

        for qt in range(4):
            n = 128 * (qt + 1)
            q0 = 128 * qt

            def ext(h, c0, c1, q0=q0):
                r = slice(64 * (h % 2), 64 * (h % 2) + 40)
                return [(CR[r, q0:q0 + 128], C1[r, h:h + 1].to_broadcast([40, c1 - c0])),
                        (C1[r, h:h + 1].to_broadcast([40, 128]), CR[r, T + c0:T + c1])]

            def done(pv, x, ob, gs, qt=qt):
                O = OB[qt % 2]
                t = finish(pv, x, ob, gs, O, None, obf[qt % 2])

                def turn_out():
                    obf[qt % 2], bt = to_B(O, qt, 0, t, qt % 2)
                    b_tok.append(bt)

                later.append([3, turn_out])

            group(lambda h, q0=q0: tuple(f(h // 2)[hsel(0, h), q0:q0 + 128] for f in (qh, ql)),
                  lambda h, a, b: tuple(f(h // 2)[hsel(0, h), a:b] for f in (kh, k2l)),
                  lambda h, q0=q0: MK[:, 384 - q0:512], [(128 * m, 128) for m in range(qt + 1)],
                  lambda h, m: FV[:, m, 64 * h:64 * h + 64], ext,
                  [f_tok, cn_tok], fv_toks, done)

        OT2 = [FQ[:, 0, :], FQ[:, 1, :]]
        ON = [FQ[:, 2, :], FQ[:, 3, :], FK[:, 0, :], FK[:, 1, :]]
        PTC = [AR[:, 6144 + 1024 * i:7168 + 1024 * i] for i in range(2)]
        onf = [None] * 4
        end_f = (PE.sem, PE.n)
        compress_end()
        ptc = [vc_tok, vc_tok]

        def compressed(qt):
            q0, u = 128 * qt, {}
            g = ai["g"]
            ai["g"] += 1
            gs, ob = g % 4, 6 + g % 2

            def scores():
                e = ai["e"] % 4
                ai["e"] += 1
                PE.wait(free[2], free[3], kc_tok, nq_tok)
                for h in range(H):
                    last = mm(bank(2 + h % 2)[:, 31 * (h // 2):31 * (h // 2) + 31], nqh(h)[:, q0:q0 + 128],
                              kcT[64 * (h % 2):64 * (h % 2) + 64, 31 * (h // 4):31 * (h // 4) + 31], True, True,
                              inc=h == H - 1)
                E = EB[e][:, 0:248].rearrange("p (h n) -> p h n", h=H)
                for w in range(2):
                    t = DV.op(C(dv.tensor_tensor, E[:, w:H:2, :],
                                bank(2 + w)[:, 0:124].rearrange("p (h n) -> p h n", h=4), BC[:, 3 - qt, w:H:2, :],
                                ALU.add), last, efree[e], bc_tok)
                    free[2 + w] = t
                t = DV.op(C(dv.tensor_reduce, nmx[gs], E, AX.X, ALU.max, negate=True), t, gfree[gs])
                t = DV.op(C(dv.tensor_tensor, E, E,
                            nmx[gs][:, :].rearrange("p (h u) -> p h u", u=1).to_broadcast([128, H, NC]), ALU.add), t)
                P = EB[e][:, 0:248]
                x = AC.op(C(ac.activation, P, P, ACT.Exp), t)
                xs = DV.op(C(dv.tensor_reduce, rsm[gs], P.rearrange("p (h n) -> p h n", h=H), AX.X, ALU.add), x)
                u.update(e=e, P=P, x=x, xs=xs)

            def turn():
                PE.wait(free[4], free[5], u["x"])
                for h in range(H):
                    last = PE.op(C(pe.transpose, PSF[0:NC, 2048 + 128 * h:2176 + 128 * h],
                                   u["P"][:, 31 * h:31 * h + 31], ident), inc=h == H - 1)
                efree[u["e"]] = [last, u["xs"]]
                pt = PTC[qt % 2]
                tk = []
                for s in range(2):
                    tk.append(AC.op(C(ac.copy, pt[0:NC, 512 * s:512 * s + 512], bank(4 + s)[0:NC, :]), last, ptc[qt % 2]))
                    free[4 + s] = tk[-1]
                u.update(pt=pt, tk=tk)

            def values():
                PE.wait(u["tk"], vc_tok, free[ob])
                for h in range(H):
                    pv = mm(bank(ob)[:, 64 * h:64 * h + 64], u["pt"][0:NC, 128 * h:128 * h + 128],
                            vcm[:, h // 4, :], True, True, inc=h == H - 1)
                ptc[qt % 2] = pv
                vg = DV.op(C(dv.tensor_scalar, GT[:, qt, :, 0], GT[:, qt, :, 0], vals[:, qt:qt + 1], None, ALU.mult),
                           gate_tok)
                onf[qt] = finish(pv, u["xs"], ob, gs, ON[qt], GT[:, qt, :, 0], [vg, (PE.sem, PE.n)])

            push({"a": scores, "b": turn, "c": values})

        ksh, ksl = halves((WH[2],)), halves((WL[2],))
        kwh, kwl = (lambda i: Bl[:, 4 + i, :]), (lambda i: Bl[:, 6 + i, :])
        n_tok = []
        for qt in range(4):
            compressed(qt)
            n_tok.append(split_to(qh(qt), ql(qt), NQ[:, qt, :], nq_tok, end_f))
            if qt < 2:
                n_tok.append(split_to(ksh(qt), ksl(qt), KS[:, qt, :], None, *ks_tok[0]))
            else:
                n_tok.append(split_to(kwh(qt - 2), kwl(qt - 2), KW[:, qt - 2, :], None, *ks_tok[1]))
        for qt in range(4):
            q0 = 128 * qt
            for br, KX, v0 in ((1, KS, 0), (2, KW, 128)):
                def done(pv, x, ob, gs, qt=qt, br=br):
                    onf[qt] = t = finish(pv, x, ob, gs, ON[qt], GT[:, qt, :, br], [onf[qt], gate_tok], first=False,
                                         tmp=OT2[br - 1])

                kx = (ksh, ksl) if br == 1 else (kwh, kwl)
                group(lambda h, q0=q0: tuple(f(h // 2)[hsel(0, h), q0:q0 + 128] for f in (qh, ql)),
                      lambda h, a, b, kx=kx: tuple(f(h // 4)[hsel(0, h), a:b] for f in kx),
                      lambda h, q0=q0: BFX[:, h, 384 - q0:512], [(128 * m, 128) for m in range(qt + 1)],
                      lambda h, m, v0=v0: V2[:, m, v0 + 64 * (h // 4):v0 + 64 * (h // 4) + 64], None,
                      [n_tok], [v2_tok], done)
        flush()
        end_a = (PE.sem, PE.n)
        split_free[:] = [end_a] * SPL
        for qt in range(4):
            AC.wait(end_a)
            _, bt = to_B(ON[qt], qt, 4, onf[qt], qt % 2)
            b_tok.append(bt)

        def merge(names, brsrc, xtok, bt, nrm):
            M = AR[:, 0:4096].rearrange("p (k t) -> p k t", k=8)
            G = [AR[:, 4096 + 512 * i:4608 + 512 * i] for i in range(4)]
            T1 = [AR[:, 6144 + 512 * i:6656 + 512 * i] for i in range(4)]
            gf, tf = [None] * 4, [None] * 4
            mt = []
            ga, gb, br, wo, bg = names
            for i in range(8):
                tt = []
                for w, nm in ((0, ga), (1, gb)):
                    b = w + 4 * (i % 2)
                    sl = 2 * (i % 2) + w
                    t = feat(nm, hA, 8, bank(b), free[b])
                    if bg is None:
                        t1 = AC.op(C(ac.activation, G[sl], bank(b), ACT.Tanh, scale=0.5), t, gf[sl])
                    else:
                        t1 = AC.op(C(ac.activation, 
                            G[sl], bank(b), ACT.Tanh, scale=0.5, bias=bg[:, 8 * w + i:8 * w + i + 1]), t, gf[sl], bg_tok)
                    free[b] = t1
                    t2 = PL.op(C(pl.tensor_scalar, G[sl], G[sl], 0.5, 0.5, ALU.mult, ALU.add), t1)
                    tt.append(t2)
                j, p = next_tile(br)
                bb = [2 + 4 * (i % 2), 3 + 4 * (i % 2)]
                PE.wait(free[bb[0]], free[bb[1]], bt)
                for w in range(2):
                    for k in range(4):
                        kk = 4 * w + k
                        a, c = WH[p][:, kk * 128:kk * 128 + 128], WL[p][:, kk * 128:kk * 128 + 128]
                        s0, e = k == 0, k == 3
                        mm(bank(bb[w]), a, Bh[:, kk, :], s0, False)
                        mm(bank(bb[w]), a, Bl[:, kk, :], False, False)
                        last = mm(bank(bb[w]), c, Bh[:, kk, :], False, e, inc=e)
                tile_done(j, last)
                for w in range(2):
                    sl = 2 * (i % 2) + w
                    tf[sl] = DV.op(C(dv.tensor_tensor, T1[sl], G[sl], bank(bb[w]), ALU.mult),
                                   last, tt[w], tf[sl])
                    gf[sl] = free[bb[w]] = tf[sl]
                s0 = 2 * (i % 2)
                t = DV.op(C(dv.tensor_tensor, M[:, i, :], T1[s0], T1[s0 + 1], ALU.add),
                          tf[s0], tf[s0 + 1])
                tf[s0] = tf[s0 + 1] = t
                mt.append(t)
            pe_done = last
            km = {}
            for k in range(8):
                km[k] = split_to(Ah[:, k, 0:T], Al[:, k, 0:T], M[:, k, :], mt[k], pe_done)
            xt = []
            for i, b, t in feats(wo, 8, hA, km):
                if i:
                    nrm.stat(i - 1, xt[i - 1])
                free[b] = t1 = DV.op(C(dv.tensor_tensor, x3[:, i, 0:T], bank(b), x3[:, i, 0:T], ALU.add),
                                     t, xtok)
                xt.append(t1)
            nrm.stat(7, xt[7])
            nrm.finish()
            return xt

        toks = queued()
        x_tok = PL.dma(x3[:, :, 0:T], d["xT"], None, toks)
        meta_tok = PL.dma(x3[:, :, T:TM], d["meta"], None)
        c2_tok = PL.dma(CS2[:, 0:296], d["cs2"], None)
        xt = merge(("ga", "gb", "br", "wo", None), hB, x_tok, b_tok, norm_to_A(T, gv[1]))

        RT = [AR[:, 4096 + 512 * i:4608 + 512 * i] for i in range(8)]
        rf = [None] * 8
        pe_b = None
        nx = norm_to_A(TM, gv[2])

        def put_x(k, src, t):
            xt[k] = t
            nx.stat(k, t, meta_tok)
            return t

        nrm = Norm(lambda k: x3[:, k, 0:T], 8, T, float(D), gv[5], put_x, NT, 6, 7, dst=lambda k: x3[:, k, 0:T],
                   held=held)
        for q in range(4):
            km = {}
            for i, b, t in feats("f1", 8, hA, hk if q == 0 else None):
                sl = 2 * (i % 4)
                free[b] = t1 = AC.op(C(ac.activation, RT[sl], bank(b), ACT.Relu), t, rf[sl])
                t2 = DV.op(C(dv.tensor_tensor, RT[sl + 1], RT[sl], RT[sl], ALU.mult), t1, rf[sl + 1])
                rf[sl] = t2
                km[i] = split_to(Bh[:, i, :], Bl[:, i, :], RT[sl + 1], t2, pe_b)
                rf[sl + 1] = km[i]
            for i in range(8):
                b = pb()
                t = feat("f2", hB, 8, bank(b), free[b], kmap=km if i == 0 else None)
                if q == 3 and i:
                    nrm.stat(i - 1, xt[i - 1])
                free[b] = xt[i] = DV.op(C(dv.tensor_tensor, x3[:, i, 0:T], bank(b), x3[:, i, 0:T],
                                                                          ALU.add), t)
            pe_b = t

        nrm.stat(7, xt[7])
        nrm.finish()

        bg_tok = DV.op(C(dv.tensor_scalar, CS2[:, 280:296], CS2[:, 280:296], 0.5, None, ALU.mult), c2_tok)
        x2_tok = PL.dma(d["x2"], x3[:, :, 0:T], None, list(xt))
        hend = nx.finish()
        kc0 = dict(hk)
        DV.wait(hend)
        AC.wait(hend)

        def v3(o, a, n):
            return AR[:, o:o + a * n].rearrange("p (a t) -> p a t", a=a)

        AQ = v3(0, 4, 512)
        QB = v3(2048, 4, 512)
        KB = v3(4096, 4, TM)
        VB = v3(6208, 4, 512)
        VBm = AR[0:NM, 8256:8768]
        BA = v3(8768, 8, 256)
        AK = v3(10816, 2, TM)
        AV = v3(11872, 4, 128)
        AVm = AR[0:NM, 12384:12512]
        IQ = v3(12512, 2, 512)
        IK = AR[:, 13536:14064]
        SCo = [14064, 14208, 14480, 14880]
        SCw = [144, 272, 400, 528]
        SMK = AR[:, 14064 + 1344:14064 + 1344 + 672].bitcast(BF)
        so = [0, 144, 416, 816]
        base = 14064 + 1344 + 672
        EB = [AR[:, base + 528 * i:base + 528 * i + 528] for i in range(4)]
        PTB = [AR[:, base + 2112 + 640 * i:base + 2112 + 640 * i + 640] for i in range(2)]
        OB = [AR[:, base + 3392:base + 3904], CTX[:, 0:512]]
        OT = CTX[:, 512:1024]
        SM = AR[:, base + 3904:20288]
        nmx = [SM[:, 8 * i:8 * i + 8] for i in range(4)]
        rsm = [SM[:, 32 + 8 * i:40 + 8 * i] for i in range(4)]
        rcp = [SM[:, 64 + 8 * i:72 + 8 * i] for i in range(4)]
        IW = SM[:, 96:112].rearrange("p (a t) -> p a t", a=4)
        mx8 = [SM[:, 112 + 8 * i:120 + 8 * i] for i in range(4)]
        BBX = XT[:, :].rearrange("p (h t) -> p h t", h=H)

        ba_tok = toep(BA, 8, 399, 256, hend)
        bb_tok = toep(BBX, 16, 127, TM, hend, x2_tok)
        t = tokmajor("ik", None, 196, (5, 3), mt=True, mbank=4)
        LN = AR[:, base:base + 640].rearrange("p (a d) -> p a d", a=5)
        mv, mq = SM[:, 144:149], SM[:, 152:157]
        r1_, r2_ = SM[:, 160:165], SM[:, 168:173]
        x_, c_ = LN[:, :, 64:128], LN[:, :, 0:64]

        def wide5(v):
            return v.rearrange("p (a u) -> p a u", u=1).to_broadcast([128, 5, 64])

        t0 = DV.op(C(dv.memset, LN[:, 4, :], 0.0), queued())
        t1 = DV.op(C(dv.tensor_copy, LN[:, 0:4, 64:128], PSA[:, 0:4, 128:192]), t)
        t1 = DV.op(C(dv.tensor_copy, LN[0:NM, 4, 64:128], PSA[0:NM, 4, 128:192]), t, t0)
        iw_tok = DV.op(C(dv.tensor_scalar, IW[:, :, :], PSA[:, 0:4, 192:196], 0.0625, None, ALU.mult), t)
        AC.op(C(ac.copy, AV[:, :, :], PSA[:, 0:4, 0:128]), t, iw_tok)
        av_tok = AC.op(C(ac.copy, AVm, PSA[0:NM, 4, 0:128]), t, iw_tok)
        for b in range(5):
            free[b] = [iw_tok, av_tok]
        t2 = DV.op(C(dv.tensor_reduce, mv, x_, AX.X, ALU.add), t1)
        t2 = DV.op(C(dv.tensor_scalar, mv, mv, -1.0 / 64, None, ALU.mult), t2)
        t2 = DV.op(C(dv.tensor_tensor, x_, x_, wide5(mv), ALU.add), t2)
        t3 = DV.op(C(dv.tensor_tensor, c_, x_, x_, ALU.mult), t2)
        t3 = DV.op(C(dv.tensor_reduce, mq, c_, AX.X, ALU.add), t3)
        t3 = DV.op(C(dv.tensor_scalar, mq, mq, 1.0 / 64, EPS, ALU.mult, ALU.add), t3)
        t3 = AC.op(C(ac.activation, r1_, mq, ACT.Ln), t3)
        t3 = AC.op(C(ac.activation, r1_, r1_, ACT.Exp, scale=-0.5), t3)
        t3 = DV.op(C(dv.tensor_tensor, r2_, r1_, r1_, ALU.mult), t3)
        t3 = DV.op(C(dv.scalar_tensor_tensor, out=r2_, in0=r2_, scalar=-0.5, in1=mq, op0=ALU.mult, op1=ALU.mult), t3)
        t3 = DV.op(C(dv.scalar_tensor_tensor, out=r1_, in0=r2_, scalar=1.5, in1=r1_, op0=ALU.add, op1=ALU.mult), t3)
        t4 = DV.op(C(dv.tensor_tensor, x_, x_, wide5(r1_), ALU.mult), t3)
        for c0, op in ((0, ALU.mult), (64, ALU.add)):
            t4 = DV.op(C(dv.tensor_tensor, x_, x_, CS2[:, c0:c0 + 64].rearrange("p (u d) -> p u d", u=1).to_broadcast(
                [128, 5, 64]), op), t4, c2_tok)
        ln_tok = DV.op(C(dv.tensor_copy, c_, x_), t4)
        for i in range(2):
            b = 5 + i
            t = feat("iq", hA, 8, bank(b), free[b])
            free[b] = iq_tok = evac(IQ[:, i, :], bank(b), 1.0, t, eng=AC)
        PE.wait(ln_tok, free[0], free[1])
        for a in range(5):
            np_ = 128 if a < 4 else NM
            last = PE.op(C(pe.transpose, PSF[:, 128 * a:128 * a + np_], LN[0:np_, a, :], ident[0:np_, 0:np_]))
        ik_tok = DV.op(C(dv.tensor_copy, IK[:, NM:TM], bank(0)), last)
        ik_tok = DV.op(C(dv.tensor_copy, IK[:, 0:NM], bank(1)[:, 0:NM]), last)
        free[0] = free[1] = ik_tok
        sc_tok = [None] * 4
        rl = [EB[2], EB[3]]
        rlf = [None, None]
        n_ = [0]
        def score(qt):
            w = SCw[qt]
            S = AR[:, SCo[qt]:SCo[qt] + w]
            tk = None
            for h in range(4):
                s = n_[0] % 2
                n_[0] += 1
                b = 2 + 2 * s
                PE.wait(free[b], free[b + 1], iq_tok, ik_tok)
                hb = 64 * (h % 2)
                for c0, c1 in ([(0, w)] if w <= T else [(0, T), (T, w)]):
                    last = mm(PSF[:, b * 512 + c0:b * 512 + c1], IQ[hb:hb + 64, h // 2, 128 * qt:128 * qt + 128],
                              IK[hb:hb + 64, c0:c1], True, True, inc=True)
                t1 = AC.op(C(ac.activation, rl[s][:, 0:w], PSF[:, b * 512:b * 512 + w], ACT.Relu),
                           last, rlf[s])
                free[b] = free[b + 1] = t1
                if h == 0:
                    tk = DV.op(C(dv.scalar_tensor_tensor, out=S[:, w - 144:w], in0=rl[s][:, w - 144:w],
                                 scalar=IW[:, qt, 0:1], in1=CS2[:, 128:272], op0=ALU.mult, op1=ALU.add),
                               t1, iw_tok, c2_tok)
                    if w > 144:
                        tk = DV.op(C(dv.tensor_scalar, S[:, 0:w - 144], rl[s][:, 0:w - 144], IW[:, qt, 0:1], None,
                                     ALU.mult), t1)
                else:
                    tk = DV.op(C(dv.scalar_tensor_tensor, 
                        out=S, in0=rl[s][:, 0:w], scalar=IW[:, qt, h:h + 1], in1=S,
                        op0=ALU.mult, op1=ALU.add), t1, tk)
                rlf[s] = tk
            sc_tok[qt] = tk

        rounds = {}

        def topk_max(qt):
            S = AR[:, SCo[qt]:SCo[qt] + SCw[qt]]
            rounds[qt] = DV.op(C(dv.max, mx8[qt], S), rounds.get(qt, sc_tok[qt]))

        def topk_drop(qt):
            S = AR[:, SCo[qt]:SCo[qt] + SCw[qt]]
            rounds[qt] = DV.op(C(dv.match_replace, S, mx8[qt], S, NREP), rounds[qt])

        def topk(qts):
            for _ in range(16):
                for fn in (topk_max, topk_drop):
                    for qt in qts:
                        idle_dv.append(lambda fn=fn, qt=qt: fn(qt))

        for qt in (3, 2, 1, 0):
            score(qt)
        topk((3, 2, 1, 0))
        b = pb()
        t = feat("bkv", hA, 8, bank(b), free[b], free[4], om=bank(4)[:, 0:NM])
        ckr = PTB[0][:, 0:TM]
        t1 = DV.op(C(dv.tensor_copy, ckr[:, 0:T], bank(b)), t)
        free[b] = t1
        t1 = DV.op(C(dv.tensor_copy, ckr[:, T:TM], bank(4)[:, 0:NM]), t)
        free[4] = t1
        bqr = VB[:, 0:2, :]
        for i in range(2):
            b = pb()
            t = feat("bq", hA, 8, bank(b), free[b])
            free[b] = bq_tok = DV.op(C(dv.tensor_copy, bqr[:, i, :], bank(b)), t)
        tmpn = AR[:, 0:6 * TM]
        ck2 = {}

        def put_ck(k, src, tt):
            ck2[0] = split_to(Bh[:, 2:4, :].rearrange("p a t -> p (a t)")[:, 0:TM],
                              Bl[:, 2:4, :].rearrange("p a t -> p (a t)")[:, 0:TM], src, tt)
            return ck2[0]

        nk_ = Norm(lambda k: ckr, 1, TM, 128.0, kvn, put_ck, tmpn, 6, 7, held=held)
        nk_.stat(0, t1)
        nk_.sums()
        bq2 = {}

        def put_bq(k, src, tt):
            bq2[k] = split_to(Bh[:, k, :], Bl[:, k, :], src, tt)
            return bq2[k]

        nq_ = Norm(lambda k: bqr[:, k, :], 2, T, 256.0, qn, put_bq, tmpn, 6, 7, held=held)
        b = pb()
        t = feat("ak", hA, 8, bank(b), free[b], free[4], om=bank(4)[:, 0:NM])
        t1 = DV.op(C(dv.tensor_copy, AK[0:64, 0, NM:TM], bank(b)[0:64, :]), t)
        t2 = DV.op(C(dv.tensor_copy, AK[64:128, 1, NM:TM], bank(b)[64:128, :]), t)
        free[b] = t2
        t1 = DV.op(C(dv.tensor_copy, AK[0:64, 0, 0:NM], bank(4)[0:64, 0:NM]), t)
        t2 = DV.op(C(dv.tensor_copy, AK[64:128, 1, 0:NM], bank(4)[64:128, 0:NM]), t)
        free[4] = t2
        nk_.scale()
        nq_.stat(0, bq_tok)
        nq_.stat(1, bq_tok)
        nq_.sums()
        ak_tok = [t2, PL.dma(AK[64:128, 0, :], AK[0:64, 0, :], None, t1), PL.dma(AK[0:64, 1, :], AK[64:128, 1, :], None, t2)]
        for i in range(4):
            b = pb()
            t = feat("aq", hA, 8, bank(b), free[b])
            if i == 0:
                nq_.scale()
            free[b] = aq_tok = evac(AQ[:, i, :], bank(b), 0.125, t, bq2[1], ck2[0], eng=AC)
        j, p = next_tile("uq")
        for i in range(4):
            b = pb()
            PE.wait(free[b], bq2[0], bq2[1])
            for k in range(2):
                a, c = WH[p][:, 512 * k + 128 * i:512 * k + 128 * i + 128], WL[p][:, 512 * k + 128 * i:512 * k + 128 * i + 128]
                mm(bank(b), a, Bh[:, k, :], k == 0, False)
                mm(bank(b), a, Bl[:, k, :], False, False)
                last = mm(bank(b), c, Bh[:, k, :], False, k == 1, inc=k == 1)
            free[b] = qb_tok = evac(QB[:, i, :], bank(b), 0.125, last, eng=AC)
        tile_done(j, last)
        j, p = next_tile("ukv")
        ckh = Bh[:, 2:4, :].rearrange("p a t -> p (a t)")
        ckl = Bl[:, 2:4, :].rearrange("p a t -> p (a t)")
        PE.wait(ck2[0])
        for i in range(4):
            b = pb()
            a, c = WH[p][:, 128 * i:128 * i + 128], WL[p][:, 128 * i:128 * i + 128]
            for o, x0, x1, bb in ((bank(b), 0, T, b), (bank(4)[:, 0:NM], T, TM, 4)):
                PE.wait(free[bb])
                mm(o, a, ckh[:, x0:x1], True, False)
                mm(o, a, ckl[:, x0:x1], False, False)
                last = mm(o, c, ckh[:, x0:x1], False, True, inc=True)
            free[b] = evac(KB[:, i, NM:TM], bank(b), 1.0, last, eng=AC)
            free[4] = kb_tok = evac(KB[:, i, 0:NM], bank(4)[:, 0:NM], 1.0, last, eng=AC)
        for a in range(5):
            b = pb()
            np_ = 128 if a < 4 else NM
            c0 = 128 * a if a < 4 else T
            wa, wb = WH[p][:, 512:1024], WL[p][:, 512:1024]
            PE.wait(free[b])
            mm(bank(b)[0:np_, :], ckh[:, c0:c0 + np_], wa, True, False)
            mm(bank(b)[0:np_, :], ckl[:, c0:c0 + np_], wa, False, False)
            last = mm(bank(b)[0:np_, :], ckh[:, c0:c0 + np_], wb, False, True, inc=True)
            free[b] = vb_tok = evac(VB[:, a, :] if a < 4 else VBm, bank(b)[0:np_, :], 1.0, last, eng=AC)
        tile_done(j, last)
        ckb_tok = last

        al_tok = [(e.sem, e.n) for e in (PE, DV, AC)]
        efree = [al_tok] * 4
        ptfree = [al_tok, al_tok]
        gfree = [None] * 4
        obf = [al_tok, al_tok]
        aqh, qbh = NH_(AQ), NH_(QB)
        kbh = NH_(KB)
        b_tok = []
        DV.wait(ba_tok, bb_tok)

        for qt in range(4):
            q0 = 128 * qt
            kst = 0 if qt == 0 else q0 - 112
            if qt == 0:
                blocks = [(0, NM), (NM, 128)]
            else:
                blocks = [(0, 128), (128, 128)]

            def vA(h, m, qt=qt):
                c = 64 * (h // 4)
                if qt == 0 and m == 0:
                    return AVm[:, c:c + 64]
                return AV[:, qt - 1 + m, c:c + 64]

            def done(pv, x, ob, gs, qt=qt):
                O = OB[qt % 2]
                sk = CS2[:, 272:280]
                wk = SM[:, 200 + 24 * (qt % 2):224 + 24 * (qt % 2)]
                t = DV.op(C(dv.tensor_tensor, wk[:, 0:8], sk, nmx[gs], ALU.add), x, c2_tok)
                t = DV.op(C(dv.tensor_scalar, wk[:, 8:16], wk[:, 0:8], 0.0, None, ALU.max), t)
                t = DV.op(C(dv.tensor_tensor, wk[:, 0:8], wk[:, 0:8], wk[:, 8:16], ALU.subtract), t)
                ta = AC.op(C(ac.activation, wk[:, 0:8], wk[:, 0:8], ACT.Exp), t)
                tb = AC.op(C(ac.activation, wk[:, 8:16], wk[:, 8:16], ACT.Exp, scale=-1.0), t)
                t = DV.op(C(dv.tensor_tensor, rsm[gs], rsm[gs], wk[:, 8:16], ALU.mult), tb, x)
                t = DV.op(C(dv.tensor_tensor, rsm[gs], rsm[gs], wk[:, 0:8], ALU.add), t, ta)
                t = finish(pv, t, ob, gs, O, wk[:, 8:16], obf[qt % 2])

                def turn_out():
                    obf[qt % 2], bt = to_B(O, qt, 0, [t, ckb_tok], qt % 2)
                    b_tok.append(bt)

                later.append([3, turn_out])

            group(lambda h, q0=q0: aqh(h)[:, q0:q0 + 128],
                  lambda h, a, b, kst=kst: AK[64 * (h % 2):64 * (h % 2) + 64, h // 4, kst + a:kst + b],
                  lambda h, qt=qt: BA[:, h, 112 if qt == 0 else 0:256], blocks, vA, None,
                  [aq_tok, ak_tok, ba_tok], [av_tok], done)
        run_idle(len(idle_dv))
        for qt in range(4):
            S = AR[:, SCo[qt]:SCo[qt] + SCw[qt]]
            sm_tok = DV.op(C(dv.tensor_scalar, SMK[:, so[qt]:so[qt] + SCw[qt]], S, -2e38, NEG,
                                                               ALU.is_gt, ALU.mult), rounds[qt])

        for qt in range(4):
            q0 = 128 * qt
            n = NM + 128 * (qt + 1)
            blocks = [(0, NM)] + [(NM + 128 * m, 128) for m in range(qt + 1)]

            def ext2(h, c0, c1, qt=qt):
                return [(IDB[:, :], SMK[:, so[qt] + c0:so[qt] + c1])]

            def done(pv, x, ob, gs, qt=qt):
                O = OB[qt % 2]
                t = finish(pv, x, ob, gs, O, None, obf[qt % 2])

                def turn_out():
                    obf[qt % 2], bt = to_B(O, qt, 4, t, qt % 2)
                    b_tok.append(bt)

                later.append([3, turn_out])

            group(lambda h, q0=q0: qbh(h)[:, q0:q0 + 128], lambda h, a, b: kbh(h)[:, a:b],
                  lambda h, q0=q0: BBX[:, h, 384 - q0:TM], blocks,
                  lambda h, m: VBm[:, 64 * h:64 * h + 64] if m == 0 else VB[:, m - 1, 64 * h:64 * h + 64],
                  ext2, [qb_tok, kb_tok, sm_tok, bb_tok, idb_tok], [vb_tok], done)
        flush()

        toks = queued()
        x_tok = PL.dma(x3[:, :, 0:T], d["x2"], None, toks, x2_tok)
        xt = merge(("ga2", "gb2", "br2", "wo2", CS2[:, 280:296]), hB, x_tok, b_tok, norm_to_A(T, gv[3]))
        rf = [None] * 8
        pe_b = None

        def put_out(k, src, t):
            return SP.dma(out[k, :, :], src, outs[k % 2], t)

        outs = [dsem("s_out0"), dsem("s_out1")]
        nrm = Norm(lambda k: x3[:, k, 0:T], 8, T, float(D), gv[4], put_out, NT, 6, 7, held=held)
        for ci, n in enumerate(SIZES2):
            km = {}
            for i in range(n):
                b = 2 * (i % 2)
                if ci == 0 and i == 0:
                    tg, tu = feat2(("fg", "fu"), hA, [bank(b), bank(b + 1)], [free[b], free[b + 1]], hk)
                else:
                    tg = feat("fg", hA, 8, bank(b), free[b])
                    tu = feat("fu", hA, 8, bank(b + 1), free[b + 1])
                sl = 2 * (i % 4)
                t1 = AC.op(C(ac.activation, RT[sl], bank(b), ACT.Tanh, scale=0.5), tg, rf[sl])
                t2 = DV.op(C(dv.scalar_tensor_tensor, 
                    out=RT[sl], in0=RT[sl], scalar=1.0, in1=bank(b), op0=ALU.add, op1=ALU.mult), t1, tg)
                free[b] = t2
                t3 = DV.op(C(dv.scalar_tensor_tensor, 
                    out=RT[sl + 1], in0=RT[sl], scalar=0.5, in1=bank(b + 1), op0=ALU.mult, op1=ALU.mult),
                    t2, tu, rf[sl + 1])
                free[b + 1] = rf[sl] = t3
                km[i] = split_to(Bh[:, i, :], Bl[:, i, :], RT[sl + 1], t3, pe_b)
                rf[sl + 1] = km[i]
            for i in range(8):
                b = pb()
                t = feat("fd", hB, n, bank(b), free[b], kmap=km if i == 0 else None)
                if ci == 2 and i:
                    nrm.stat(i - 1, xt[i - 1])
                free[b] = xt[i] = DV.op(C(dv.tensor_tensor, x3[:, i, 0:T], bank(b), x3[:, i, 0:T],
                                                                          ALU.add), t)
            pe_b = t
        nrm.stat(7, xt[7])
        nrm.finish()
        PL.wait((outs[0][0], outs[0][1]), (outs[1][0], outs[1][1]))
        assert st["use"] == len(tiles)

        with nc.Block() as block:
            for q, reg in ((SP, block.sync), (PE, block.tensor), (DV, block.vector), (AC, block.scalar),
                           (PL, block.gpsimd)):
                def run(e, q=q):
                    for fn in q.q:
                        fn()
                reg(run)


def columns(w, c0, n=128):
    k = w.shape[0] // 128
    return w[:, c0:c0 + n].reshape(k, 128, n).transpose(1, 0, 2).reshape(128, k * n)


def rows(w, k0, nk):
    n = w.shape[1]
    return w[128 * k0:128 * (k0 + nk)].reshape(nk, 128, n).transpose(1, 0, 2).reshape(128, nk * n)


def bucket(n):
    large = 16 + (np.log(np.maximum(n, 16) / 16.0) / np.log(8.0) * 16).astype(np.int64)
    return np.where(n < 16, n, np.minimum(large, 31))


def one_hot(dist):
    o = np.zeros((34, dist.size), np.float32)
    ok = dist >= 0
    o[bucket(np.maximum(dist, 0))[ok], np.nonzero(ok)[0]] = 1.0
    o[32, ~ok] = NEG
    o[33, dist >= 128] = NEG
    return o


def layout(a):
    w_in, w2 = a["w_in"][0], a["w_in_2"][0]
    tiles = tile_list()
    pack = np.zeros((len(tiles), 128, 1024), np.float32)
    a2 = np.concatenate([w_in[:, 2440:2568], w_in[:, 2696:2824], w_in[:, 1536:1544], w_in[:, 2824:2848]], axis=1)
    ik = np.concatenate([w2[:, 640:768], w2[:, 1408:1472], w2[:, 1472:1476]], axis=1)
    col = {"fq": (w_in, 0), "fk": (w_in, 512), "nq": (w_in, 1544), "ga": (w_in, 2848), "gb": (w_in, 3872),
           "wo": (a["w_out"][0], 0), "f1": (a["w_ff1"][0], 0), "aq": (w2, 0), "bq": (w2, 768), "bkv": (w2, 1024),
           "iq": (w2, 1152), "ak": (w2, 512), "ga2": (w2, 1476), "gb2": (w2, 2500), "wo2": (a["w_out_2"][0], 0),
           "fg": (a["w_ffn_gate_2"][0], 0), "fu": (a["w_ffn_up_2"][0], 0)}
    kv = (2056, 2184, 2312, 2568)
    for j, (name, i, n, _) in enumerate(tiles):
        if name in col:
            w, c0 = col[name]
            t = columns(w, c0 + 128 * i)
        elif name == "kv":
            t = columns(w_in, kv[i])
        elif name == "fv":
            t = rows(w_in[:, 1024:1536], 2 * i, 2)
        elif name == "a2":
            t = rows(a2, 3 * i, n // 288)
        elif name == "ik":
            t = rows(ik, 5 * i, n // 196)
        elif name in ("w1k", "w1v"):
            t = rows(a["cmp_w1_k" if name == "w1k" else "cmp_w1_v"][0], 4 * i, 4)
        elif name == "br":
            t = np.concatenate([columns(a["w_br_fox"][0], 128 * i), columns(a["w_br_nsa"][0], 128 * i)], axis=1)
        elif name == "br2":
            t = np.concatenate([columns(a["w_branch_a_2"][0], 128 * i), columns(a["w_branch_b_2"][0], 128 * i)],
                               axis=1)
        elif name == "f2":
            q, f = divmod(i, 8)
            t = columns(a["w_ff2"][0][1024 * q:1024 * q + 1024], 128 * f)
        elif name == "fd":
            c, f = divmod(i, 8)
            t = columns(a["w_ffn_down_2"][0][1024 * c:1024 * c + n], 128 * f)
        elif name == "uq":
            t = rows(a["w_uq_2"][0], 0, 2)
        else:
            t = np.concatenate([a["w_uk_2"][0].reshape(128, 512), a["w_uv_2"][0].reshape(128, 512)], axis=1)
        pack[j, :, 0:n] = t

    def chunks(v):
        return v.reshape(-1, 128).transpose(1, 0)

    def fm(x):
        return np.ascontiguousarray(x.reshape(x.shape[0], 8, 128).transpose(2, 1, 0))

    cst = np.zeros((128, 196), np.float32)
    cst[:, 0:128] = np.eye(128)
    for i, g in enumerate((a["g_attn"][0], a["g_mlp"][0], a["attn_norm_g_2"][0], a["ffn_norm_g_2"][0],
                           a["final_norm_g_2"], a["g_final"])):
        cst[:, 128 + 8 * i:136 + 8 * i] = chunks(g)
    for r in (0, 32, 64, 96):
        cst[r:r + 8, 178:186] = np.eye(8)
        cst[r:r + 8, 186] = a["b_forget"][0]
    cst[:, 187:191] = 1.0
    cst[0:31, 187] = 0.0
    cst[:, 192:194] = chunks(a["q_norm_g_2"][0])
    cst[:, 194:195] = chunks(a["kv_norm_g_2"][0])
    cs1 = np.zeros((128, 416), np.float32)
    cs1[:, 0:16] = chunks(a["cmp_pe_k"][0].reshape(-1))
    cs1[:, 16:32] = chunks(a["cmp_pe_v"][0].reshape(-1))
    for c in range(2):
        w = a["cmp_w2_k"][0][128 * c:128 * c + 128]
        cs1[:, 32 + 128 * c:96 + 128 * c] = w
        cs1[:, 96 + 128 * c:160 + 128 * c] = w
        cs1[:, 288 + 64 * c:352 + 64 * c] = a["cmp_w2_v"][0][128 * c:128 * c + 128]
    cs2 = np.zeros((128, 296), np.float32)
    cs2[:, 0:64] = a["idx_k_ln_g_2"][0]
    cs2[:, 64:128] = a["idx_k_ln_b_2"][0]
    q, j = np.arange(128)[:, None], np.arange(144)[None, :]
    cs2[:, 128:272] = np.where(j > 16 + q, np.float32(NADM), np.float32(0.0))
    cs2[:, 272:280] = a["sinks_2"][0]
    cs2[:, 280:296] = chunks(a["b_gates_2"][0])
    mk = np.where(np.arange(T)[None, :] - 384 > q, np.float32(NEG), np.float32(0.0))
    tab = np.zeros((34, 24), np.float32)
    tab[0:32, 0:8] = a["rel_bias_table"]
    tab[0:32, 8:24] = a["rel_bias_2"]
    tab[32] = 1.0
    tab[33, 8:16] = 1.0
    return {"w": pack, "xT": fm(a["x"][0]), "meta": fm(a["meta_tokens_2"]), "cst": cst, "cs1": cs1, "cs2": cs2,
            "mk": mk, "tab": tab, "ohf": one_hot((465 + np.arange(16)[:, None] - 16 * np.arange(62)[None, :]).reshape(-1)), "ohr": one_hot(527 - np.arange(NR_))}


def kernel(**inputs):
    import concourse.bacc as bacc
    from concourse.bass_utils import run_bass_kernel_spmd

    arrays = layout({k: np.asarray(v) for k, v in inputs.items()})
    nc = bacc.Bacc("TRN2", target_bir_lowering=False, num_devices=1)
    d = {k: nc.dram_tensor(k + "_in", v.shape, F, kind="ExternalInput").ap() for k, v in arrays.items()}
    d["scr"] = nc.dram_tensor("scr_tmp", (24, 16, NR_), F, kind="Internal").ap()
    d["scr2"] = nc.dram_tensor("scr2_tmp", (31968,), F, kind="Internal").ap()
    d["x2"] = nc.dram_tensor("x2_tmp", (128, 8, T), F, kind="Internal").ap()
    out = nc.dram_tensor("out_0", (8, 128, T), F, kind="ExternalOutput").ap()
    build(nc, d, out)
    r = run_bass_kernel_spmd(nc, [{k + "_in": v for k, v in arrays.items()}], core_ids=[0])
    y = r.results[0]["out_0"]
    return np.ascontiguousarray(y.reshape(D, T).transpose(1, 0)).reshape(1, T, D)
```
